# Optimizing a Trainium2 kernel written in Bass

```python
import jax, jax.numpy as jnp
from jax import lax
import numpy as np

D_MODEL = 1024
BATCH = 1
SEQ = 512
DEPTH = 2
DEC_BATCH = 8
DEC_SEQ = 16
PAST_LEN = 1024

CHUNK = 64
A_HEADS = 16
A_HEAD_DIM = 64
A_WIDTH = A_HEADS * A_HEAD_DIM
A_DECAY_RANK = 64
A_ICLR_RANK = 64
A_GATE_RANK = 128
A_COLS = 3 * A_WIDTH + A_DECAY_RANK + A_ICLR_RANK + A_GATE_RANK
A_GN_EPS = 64e-5
B_HEADS = 4
B_KEY_DIM = 256
B_VAL_DIM = 512
B_QK_WIDTH = B_HEADS * B_KEY_DIM
B_V_WIDTH = B_HEADS * B_VAL_DIM
B_COLS = 2 * B_QK_WIDTH + 2 * B_V_WIDTH
GATE_COLS = 2 * D_MODEL
IN_COLS = A_COLS + B_COLS + GATE_COLS
FFN_HIDDEN = 4 * D_MODEL
ROPE_BASE = 10000.0
NORM_EPS = 1e-6

kernel_name = 'hybrid_rwkv7_retention_streaming_encoder_step'

def _rms_norm(x, g):
    xf = x.astype(jnp.float32)
    y = xf * lax.rsqrt(jnp.mean(xf * xf, axis=-1, keepdims=True) + NORM_EPS)
    return (y * g.astype(jnp.float32)).astype(x.dtype)

def _rope(x, pos):
    half = x.shape[-1] // 2
    inv_freq = ROPE_BASE ** (-jnp.linspace(0.0, 1.0, half, dtype=jnp.float32))
    ang = pos.astype(jnp.float32)[:, None] * inv_freq[None, :]
    cos = jnp.cos(ang)[None, :, None, :]
    sin = jnp.sin(ang)[None, :, None, :]
    x1, x2 = x[..., :half], x[..., half:]
    return jnp.concatenate([x1 * cos - x2 * sin, x1 * sin + x2 * cos], axis=-1)

def _rwkv7_step(S, inp):
    r, w, k, v, a, b = inp
    sa = jnp.einsum('bhvk,bhk->bhv', S, a)
    S = S * w[:, :, None, :] + sa[..., None] * b[:, :, None, :] + v[..., None] * k[:, :, None, :]
    y = jnp.einsum('bhvk,bhk->bhv', S, r)
    return S, y

def _rwkv7_branch(za, s0, p):
    bsz, t, _ = za.shape
    za = za.astype(jnp.float32)
    r, k, v, zw, zi, zg = jnp.split(
        za, [A_WIDTH, 2 * A_WIDTH, 3 * A_WIDTH, 3 * A_WIDTH + A_DECAY_RANK,
             3 * A_WIDTH + A_DECAY_RANK + A_ICLR_RANK], axis=-1)
    w_log = -jax.nn.softplus(-(p['a_w0'] + jnp.tanh(zw) @ p['a_w2'])) - 0.5
    decay = jnp.exp(-jnp.exp(w_log))
    iclr = jax.nn.sigmoid(p['a_a0'] + zi @ p['a_a2'])
    gate = jax.nn.sigmoid(zg) @ p['a_g2']
    kk = (k * p['a_kk']).reshape(bsz, t, A_HEADS, A_HEAD_DIM)
    kk = kk / jnp.maximum(jnp.sqrt(jnp.sum(kk * kk, axis=-1, keepdims=True)), 1e-12)
    k = k * (1.0 + (iclr - 1.0) * p['a_ka'])
    r_h = r.reshape(bsz, t, A_HEADS, A_HEAD_DIM)
    k_h = k.reshape(bsz, t, A_HEADS, A_HEAD_DIM)
    v_h = v.reshape(bsz, t, A_HEADS, A_HEAD_DIM)
    w_h = decay.reshape(bsz, t, A_HEADS, A_HEAD_DIM)
    i_h = iclr.reshape(bsz, t, A_HEADS, A_HEAD_DIM)
    xs = tuple(jnp.moveaxis(u, 1, 0) for u in (r_h, w_h, k_h, v_h, -kk, kk * i_h))
    s_new, y = lax.scan(_rwkv7_step, s0.astype(jnp.float32), xs)
    y = jnp.moveaxis(y, 0, 1)
    mu = jnp.mean(y, axis=-1, keepdims=True)
    var = jnp.mean(jnp.square(y - mu), axis=-1, keepdims=True)
    y = (y - mu) * lax.rsqrt(var + A_GN_EPS)
    y = y * p['a_ln_w'].reshape(A_HEADS, A_HEAD_DIM) + p['a_ln_b'].reshape(A_HEADS, A_HEAD_DIM)
    bonus = jnp.sum(r_h * k_h * p['a_rk'], axis=-1, keepdims=True) * v_h
    out = (y + bonus).reshape(bsz, t, A_WIDTH) * gate
    return out, s_new

def _retention_log_decay():
    return jnp.log(1.0 - 2.0 ** (-5.0 - jnp.arange(B_HEADS, dtype=jnp.float32)))

def _retention_chunk(S, inp):
    q, k, v = inp
    c = q.shape[2]
    log_g = _retention_log_decay()
    idx = jnp.arange(c, dtype=jnp.float32)
    diff = idx[:, None] - idx[None, :]
    mask = jnp.where(diff >= 0.0, jnp.exp(jnp.maximum(diff, 0.0)[None] * log_g[:, None, None]), 0.0)
    scores = jnp.einsum('bhid,bhjd->bhij', q, k) * mask
    inner = jnp.einsum('bhij,bhjv->bhiv', scores, v)
    q_dec = q * jnp.exp((idx + 1.0)[None, :] * log_g[:, None])[None, :, :, None]
    cross = jnp.einsum('bhid,bhdv->bhiv', q_dec, S)
    k_dec = k * jnp.exp((c - 1.0 - idx)[None, :] * log_g[:, None])[None, :, :, None]
    S = S * jnp.exp(c * log_g)[None, :, None, None] + jnp.einsum('bhjd,bhjv->bhdv', k_dec, v)
    return S, inner + cross

def _retention_branch(zb, s0, pos):
    bsz, t, _ = zb.shape
    zb = zb.astype(jnp.float32)
    q, k, v, g = jnp.split(zb, [B_QK_WIDTH, 2 * B_QK_WIDTH, 2 * B_QK_WIDTH + B_V_WIDTH], axis=-1)
    q = _rope(q.reshape(bsz, t, B_HEADS, B_KEY_DIM), pos)
    k = _rope(k.reshape(bsz, t, B_HEADS, B_KEY_DIM), pos) * (B_KEY_DIM ** -0.5)
    v = v.reshape(bsz, t, B_HEADS, B_VAL_DIM)
    c = CHUNK if t % CHUNK == 0 else t
    nc = t // c

    def blocks(u):
        return jnp.transpose(u.reshape(bsz, nc, c, B_HEADS, u.shape[-1]), (1, 0, 3, 2, 4))

    s_new, y = lax.scan(_retention_chunk, s0.astype(jnp.float32), (blocks(q), blocks(k), blocks(v)))
    y = jnp.transpose(y, (1, 0, 3, 2, 4)).reshape(bsz, t, B_HEADS, B_VAL_DIM)
    y = y * lax.rsqrt(jnp.mean(y * y, axis=-1, keepdims=True) + NORM_EPS)
    out = jax.nn.silu(g) * y.reshape(bsz, t, B_V_WIDTH)
    return out, s_new

def _token_mixer(h, shift_prev, s_rwkv, s_ret, pos, p):
    bsz, t, _ = h.shape
    z = h @ p['w_in']
    za, zb, zg = jnp.split(z, [A_COLS, A_COLS + B_COLS], axis=-1)
    za_prev = jnp.concatenate([shift_prev[:, None, :].astype(za.dtype), za[:, :-1]], axis=1)
    za_mix = za + (za_prev - za) * p['a_mu']
    y_a, new_rwkv = _rwkv7_branch(za_mix, s_rwkv, p)
    y_b, new_ret = _retention_branch(zb, s_ret, pos)
    gates = jax.nn.sigmoid(zg.astype(jnp.float32)).reshape(bsz, t, 2, D_MODEL)
    merged = (gates[:, :, 0] * (y_a.astype(h.dtype) @ p['w_branch_a'])
              + gates[:, :, 1] * (y_b.astype(h.dtype) @ p['w_branch_b']))
    out = merged.astype(h.dtype) @ p['w_out']
    return out, za[:, -1], new_rwkv, new_ret

def _layer(x, c, shift_prev, s_rwkv, s_ret, pos, p):
    mod = jax.nn.silu(c) @ p['ada_w'] + p['ada_b']
    sh1, sc1, gt1, sh2, sc2, gt2 = [u[:, None, :] for u in jnp.split(mod, 6, axis=-1)]
    h = (_rms_norm(x, p['norm_pre'][0]) * (1.0 + sc1) + sh1).astype(x.dtype)
    mix, new_shift, new_rwkv, new_ret = _token_mixer(h, shift_prev, s_rwkv, s_ret, pos, p)
    x = (x + gt1 * _rms_norm(mix, p['norm_post'][0])).astype(x.dtype)
    h = (_rms_norm(x, p['norm_pre'][1]) * (1.0 + sc2) + sh2).astype(x.dtype)
    f = jnp.square(jax.nn.relu(h @ p['w_ffn_up'])) @ p['w_ffn_down']
    x = (x + gt2 * _rms_norm(f, p['norm_post'][1])).astype(x.dtype)
    return x, new_shift, new_rwkv, new_ret

def setup_inputs(seed: int = 0) -> dict:
    key = jax.random.key(seed)
    ks = jax.random.split(key, 32)
    f32 = jnp.float32

    def nrm(i, shape, scale):
        return jax.random.normal(ks[i], shape, f32) * scale

    return {
        'x_prompt': nrm(0, (BATCH, SEQ, D_MODEL), 1.0),
        'x_sample': nrm(1, (DEC_BATCH, DEC_SEQ, D_MODEL), 1.0),
        'state_shift': nrm(2, (DEPTH, DEC_BATCH, A_COLS), 1.0),
        'state_rwkv': nrm(3, (DEPTH, DEC_BATCH, A_HEADS, A_HEAD_DIM, A_HEAD_DIM), 0.3),
        'state_ret': nrm(4, (DEPTH, DEC_BATCH, B_HEADS, B_KEY_DIM, B_VAL_DIM), 0.3),
        'c_prompt': nrm(5, (BATCH, D_MODEL), 1.0),
        'c_sample': nrm(6, (DEC_BATCH, D_MODEL), 1.0),
        'ada_w': nrm(7, (DEPTH, D_MODEL, 6 * D_MODEL), 0.5 * D_MODEL ** -0.5),
        'ada_b': nrm(8, (DEPTH, 6 * D_MODEL), 0.02),
        'norm_pre': 1.0 + nrm(9, (DEPTH, 2, D_MODEL), 0.02),
        'norm_post': 1.0 + nrm(10, (DEPTH, 2, D_MODEL), 0.02),
        'w_in': nrm(11, (DEPTH, D_MODEL, IN_COLS), D_MODEL ** -0.5),
        'a_mu': jax.random.uniform(ks[12], (DEPTH, A_COLS), f32, 0.0, 1.0),
        'a_w0': jax.random.uniform(ks[13], (DEPTH, A_WIDTH), f32, -6.0, -1.0),
        'a_w2': nrm(14, (DEPTH, A_DECAY_RANK, A_WIDTH), 0.1),
        'a_a0': nrm(15, (DEPTH, A_WIDTH), 0.1),
        'a_a2': nrm(16, (DEPTH, A_ICLR_RANK, A_WIDTH), 0.5 * A_ICLR_RANK ** -0.5),
        'a_g2': nrm(17, (DEPTH, A_GATE_RANK, A_WIDTH), A_GATE_RANK ** -0.5),
        'a_kk': 0.85 + nrm(18, (DEPTH, A_WIDTH), 0.05),
        'a_ka': 1.0 + nrm(19, (DEPTH, A_WIDTH), 0.05),
        'a_rk': nrm(20, (DEPTH, A_HEADS, A_HEAD_DIM), 0.1),
        'a_ln_w': 1.0 + nrm(21, (DEPTH, A_WIDTH), 0.02),
        'a_ln_b': nrm(22, (DEPTH, A_WIDTH), 0.02),
        'w_branch_a': nrm(23, (DEPTH, A_WIDTH, D_MODEL), A_WIDTH ** -0.5),
        'w_branch_b': nrm(24, (DEPTH, B_V_WIDTH, D_MODEL), B_V_WIDTH ** -0.5),
        'w_out': nrm(25, (DEPTH, D_MODEL, D_MODEL), D_MODEL ** -0.5),
        'w_ffn_up': nrm(26, (DEPTH, D_MODEL, FFN_HIDDEN), D_MODEL ** -0.5),
        'w_ffn_down': nrm(27, (DEPTH, FFN_HIDDEN, D_MODEL), FFN_HIDDEN ** -0.5),
    }

def reference(x_prompt, x_sample, state_shift, state_rwkv, state_ret, c_prompt, c_sample,
              ada_w, ada_b, norm_pre, norm_post, w_in, a_mu, a_w0, a_w2, a_a0, a_a2, a_g2,
              a_kk, a_ka, a_rk, a_ln_w, a_ln_b, w_branch_a, w_branch_b, w_out, w_ffn_up, w_ffn_down):
    t_p = x_prompt.shape[1]
    t_s = x_sample.shape[1]
    bp = x_prompt.shape[0]
    pos_p = jnp.arange(t_p, dtype=jnp.int32)
    pos_s = PAST_LEN + jnp.arange(t_s, dtype=jnp.int32)
    zero_shift = jnp.zeros((bp, A_COLS), x_prompt.dtype)
    zero_rwkv = jnp.zeros((bp, A_HEADS, A_HEAD_DIM, A_HEAD_DIM), jnp.float32)
    zero_ret = jnp.zeros((bp, B_HEADS, B_KEY_DIM, B_VAL_DIM), jnp.float32)

    xp = x_prompt
    xs = x_sample
    shift_p, rwkv_p, ret_p = [], [], []
    shift_s, rwkv_s, ret_s = [], [], []
    for l in range(DEPTH):
        p = {
            'ada_w': ada_w[l], 'ada_b': ada_b[l], 'norm_pre': norm_pre[l], 'norm_post': norm_post[l],
            'w_in': w_in[l], 'a_mu': a_mu[l], 'a_w0': a_w0[l], 'a_w2': a_w2[l], 'a_a0': a_a0[l],
            'a_a2': a_a2[l], 'a_g2': a_g2[l], 'a_kk': a_kk[l], 'a_ka': a_ka[l], 'a_rk': a_rk[l],
            'a_ln_w': a_ln_w[l], 'a_ln_b': a_ln_b[l], 'w_branch_a': w_branch_a[l],
            'w_branch_b': w_branch_b[l], 'w_out': w_out[l], 'w_ffn_up': w_ffn_up[l],
            'w_ffn_down': w_ffn_down[l],
        }
        xp, sp, rp, tp = _layer(xp, c_prompt, zero_shift, zero_rwkv, zero_ret, pos_p, p)
        xs, ss, rs, ts = _layer(xs, c_sample, state_shift[l], state_rwkv[l], state_ret[l], pos_s, p)
        shift_p.append(sp)
        rwkv_p.append(rp)
        ret_p.append(tp)
        shift_s.append(ss)
        rwkv_s.append(rs)
        ret_s.append(ts)

    new_shift_prompt = jnp.stack(shift_p).astype(state_shift.dtype)
    new_rwkv_prompt = jnp.stack(rwkv_p).astype(state_rwkv.dtype)
    new_ret_prompt = jnp.stack(ret_p).astype(state_ret.dtype)
    new_shift_sample = jnp.stack(shift_s).astype(state_shift.dtype)
    new_rwkv_sample = jnp.stack(rwkv_s).astype(state_rwkv.dtype)
    new_ret_sample = jnp.stack(ret_s).astype(state_ret.dtype)
    return (xp, xs, new_shift_prompt, new_rwkv_prompt, new_ret_prompt,
            new_shift_sample, new_rwkv_sample, new_ret_sample)


_drawn_inputs = setup_inputs


def setup_inputs(seed=0):
    import zlib

    import numpy as np

    out = dict(_drawn_inputs(seed))
    spreads = {}
    factors = {'norm_post': 4.794, 'a_ln_w': 8.0, 'a_ln_b': 8.0}
    for name, (base, spread) in spreads.items():
        noise = np.random.default_rng([zlib.crc32(name.encode()), seed]).standard_normal(out[name].shape)
        drawn = base * np.exp(spread * noise) if base else spread * noise
        out[name] = __import__('jax').numpy.asarray(drawn.astype(out[name].dtype))
    for name, factor in factors.items():
        out[name] = (out[name] * factor).astype(out[name].dtype)
    return out
```

```python
import numpy as np
import concourse.bass as bass
from concourse import mybir
from contextlib import ExitStack

F32 = mybir.dt.float32
F32R = mybir.dt.float32r
ACT = mybir.ActivationFunctionType
ALU = mybir.AluOpType

D = 1024
DEPTH = 2
SEQ, DEC_B, DEC_T, PAST = 512, 8, 16, 1024
TOK = SEQ + DEC_B * DEC_T
HALF = TOK // 2
NBLK = TOK // 128
PB = SEQ // 128
KD = D // 128
A_COLS, B_COLS = 3328, 6144
A_T = A_COLS // 128
PAIRS = 8
RH, RK, RV = 4, 256, 512
FFN = 4 * D
LEVELS = 7
S_LEVELS = 4
EPS, GN_EPS = 1e-6, 64e-5
NSTREAM = 1 + DEC_B

SCR = 20500

C_ID, C_BD, C_ONE = 0, 128, 256
C_SU, C_SUS, C_IU, C_IUS = 384, 512, 640, 768
C_LM = 896
C_LMT = C_LM + 128 * LEVELS
C_HM = C_LMT + 128
C_BM = C_HM + 2
C_RM = C_BM + DEC_B
C_E8 = C_RM + TOK
NC1 = C_E8 + DEC_B * DEC_B
K_COS, K_SIN = 0, TOK
K_MW = 2 * TOK
K_MS = K_MW + RH * SEQ
K_QD = K_MS + RH * 128
K_KP = K_QD + RH * 128
K_KS = K_KP + RH * PB
NC2 = K_KS + RH * DEC_B


def shape_constants():
    i = np.arange(128)
    c = np.zeros((128, NC1), np.float32)
    c[:, C_ID:C_ID + 128] = np.eye(128)
    c[:, C_BD:C_BD + 128] = (i[:, None] // 64) == (i[None, :] // 64)
    c[:, C_ONE:C_ONE + 128] = 1
    same = (i[:, None] // DEC_T) == (i[None, :] // DEC_T)
    lt, le = i[:, None] < i[None, :], i[:, None] <= i[None, :]
    c[:, C_SU:C_SU + 128], c[:, C_SUS:C_SUS + 128] = lt, lt & same
    c[:, C_IU:C_IU + 128], c[:, C_IUS:C_IUS + 128] = le, le & same
    for lv in range(LEVELS):
        m = 1 << lv
        low = (i[:, None] // (2 * m) == i[None, :] // (2 * m)) & (i[:, None] // m % 2 == 1) & (i[None, :] // m % 2 == 0)
        c[:, C_LM + 128 * lv:C_LM + 128 * lv + 128] = low | np.eye(128, dtype=bool)
        if lv == 0:
            c[:, C_LMT:C_LMT + 128] = (low | np.eye(128, dtype=bool)).T
    c[:, C_HM] = i < 64
    c[:, C_HM + 1] = i >= 64
    for b in range(DEC_B):
        c[:, C_BM + b] = i // DEC_T == b
    reset = np.ones(TOK, np.float32)
    reset[0:SEQ:128] = 0
    reset[SEQ::DEC_T] = 0
    c[:, C_RM:C_RM + TOK] = reset
    c[:, C_E8:C_E8 + DEC_B * DEC_B] = np.eye(DEC_B).reshape(-1)
    k = np.zeros((128, NC2), np.float32)
    inv = np.float32(10000.0) ** (-np.linspace(0.0, 1.0, RK // 2, dtype=np.float32))
    pos = np.concatenate([np.arange(SEQ), PAST + np.tile(np.arange(DEC_T), DEC_B)]).astype(np.float32)
    ang = (inv.astype(np.float32)[:, None] * pos[None, :]).astype(np.float32).astype(np.float64)
    k[:, K_COS:K_COS + TOK], k[:, K_SIN:K_SIN + TOK] = np.cos(ang), np.sin(ang)
    scale = float(RK) ** -0.5
    for h in range(RH):
        g = 1.0 - 2.0 ** (-5.0 - h)
        d = np.arange(SEQ)[None, :] - i[:, None]
        k[:, K_MW + SEQ * h:K_MW + SEQ * (h + 1)] = np.where(d >= 0, g ** np.maximum(d, 0), 0) * scale
        d = i[None, :] - i[:, None]
        k[:, K_MS + 128 * h:K_MS + 128 * (h + 1)] = np.where((d >= 0) & same, g ** np.maximum(d, 0), 0) * scale
        k[:, K_QD + 128 * h:K_QD + 128 * (h + 1)] = g ** (i % DEC_T + 1.0)
        for b in range(PB):
            k[:, K_KP + PB * h + b] = g ** (SEQ - 1.0 - (128 * b + i)) * scale
        for b in range(DEC_B):
            k[:, K_KS + DEC_B * h + b] = np.where(i // DEC_T == b, g ** (DEC_T - 1.0 - i % DEC_T), 0) * scale
    return c, k


Z_TILES = 6
SPILLED = PAIRS * Z_TILES + 3 * (PAIRS - 1)

POINTS = [("sq", 3), ("rk", 3), ("ab", 4), ("z", 1), ("lti", 1)]
POINTS += [(f"{w}{lv}", 1) for lv in range(1, LEVELS) for w in ("la", "lb")]
POINTS += [("uw", 1)] + [(f"{w}{c}", 1) for c in range(PB) for w in ("ca", "cb")]
POINTS += [("su", 1), ("sn", 1), ("so", 1), ("gn", 2), ("end", 99)]


def filler(l, p):
    out = []
    start = number_jobs()[0]
    for i in range(Z_TILES):
        t = Z_TILES * p + i
        out.append((start[l, f"z{p}"] + i, t, t % 12 >= 8))
    if p < PAIRS - 1:
        out += [(start[l, f"rkv{p + 1}"] + i, PAIRS * Z_TILES + 3 * p + i, False) for i in range(3)]
    return out


def spill_number(l, p, i):
    return l * SPILLED + p * (Z_TILES + 3) + i


def jobs_of_layer():
    jobs = [("lora", 2, 8, "a"), ("rkv0", 3, 8, "a")]
    for p in range(PAIRS):
        jobs.append((f"z{p}", Z_TILES, 8, "a"))
        if p < PAIRS - 1:
            jobs.append((f"rkv{p + 1}", 3, 8, "a"))
        if p % 4 == 3:
            jobs.append((f"ba{p // 4}", 8, 4, "v"))
    jobs.append(("gate0", 8, 8, "a"))
    for h in range(RH):
        jobs.append((f"bb{h}", 8, 4, "v"))
    jobs.append(("gate1", 8, 8, "a"))
    jobs.append(("out0", 8, 4, "v"))
    jobs.append(("out1", 8, 4, "v"))
    for f in range(8):
        jobs.append((f"up{f}", 4, 8, "a"))
        jobs.append((f"down{f}", 8, 4, "v"))
    return jobs


def number_jobs():
    start, freed_by, kt = {}, [], []
    for l in range(DEPTH):
        for name, n, k, by in jobs_of_layer():
            start[l, name] = len(freed_by)
            freed_by += [by] * n
            kt += [k] * n
    return start, freed_by, kt


def rw_groups(lv):
    return (0, 1, 2) if lv < S_LEVELS else (0, 1)


RET_PE = ["tr"] + [f"s{b}" for b in range(NBLK)] + ["sp"] + [f"ss{b}" for b in range(DEC_B)] + ["rn"]
RET_VE = ["rope", "ks"] + [f"p{b}" for b in range(NBLK)] + ["qx"] + [f"ss{b}" for b in range(DEC_B)] + ["var", "y", "split"]
RET_AC = ["vk", "sp", "y", "ysq", "sd", "hi"]


def rw_pe():
    out = ["wi", "ss", "bs"] + [f"t{b}" for b in range(NBLK)] + [f"s{j}" for j in range(2 * NBLK)] + ["z"]
    out += [f"lt{g}" for g in range(3)]
    for lv in range(1, LEVELS):
        out += [f"T{lv}.{g}" for g in rw_groups(lv)]
        out += [f"{w}{lv}.{g}" for g in rw_groups(lv) for w in ("X", "XT")]
    out += ["uw", "sT"]
    for c in range(PB):
        out += [f"u{c}"] * (c > 0) + [f"new{c}"]
    return out + ["spo", "su", "y", "snew", "sout", "gn1", "gate", "gn2"]


def rw_ve():
    out = ["mix", "sq", "rk", "bo", "ea", "abkr"] + [f"s{j}" for j in range(2 * NBLK)] + ["lti", "x0.0", "x0.1", "x0.2"]
    for lv in range(1, LEVELS):
        out += [f"T{lv}.{g}" for g in rw_groups(lv)]
    for c in range(PB):
        out += [f"ss{c}"] * (c > 0) + [f"u{c}", f"new{c}"]
    return out + ["wm", "smask", "su", "snew", "yc", "var", "y", "split"]


def rw_ac():
    out = ["sig", "nr", "ea", "exp"] + [f"t{b}" for b in range(NBLK)] + ["z"]
    for lv in range(1, LEVELS):
        out += [f"{w}{lv}.{g}" for g in rw_groups(lv) for w in ("X", "XT")]
    return out + ["uw", "sT", "spo", "y", "sout", "gate", "sd", "hi"]


def count_marks(head, rw, ba, ret, tail):
    out = []
    for l in range(DEPTH):
        out += [(l, n) for n in head(l)]
        for p in range(PAIRS):
            out += [(l, "rw", p, n) for n in rw]
        for h in range(RH):
            out += [(l, "rt", h, n) for n in ret]
        out += [(l, n) for n in tail(l)]
    assert len(set(out)) == len(out)
    return {k: n + 1 for n, k in enumerate(out)}


def marks_pe():
    return count_marks(lambda l: ["par", "ct"] + [f"x{b}" for b in range(NBLK)] * (l == 0) + ["n0"], rw_pe(), 0, RET_PE,
                       lambda l: ["nsh", "mix", "n1", "ffn"] + [f"o{b}" for b in range(NBLK)] * (l == DEPTH - 1))


def marks_ve():
    return count_marks(lambda l: ["mod", "var0", "hx0", "h0", "lora"], rw_ve(), 0, RET_VE,
                       lambda l: ["ms0", "ms1", "varm", "x1", "var1", "hx1", "h1", "varf", "x2"])


def marks_ac():
    return count_marks(lambda l: ["silu", "par", "ct"] + [f"x{b}" for b in range(NBLK)] * (l == 0) + ["mod", "sq0", "sd0", "hi0", "lora"],
                       rw_ac(), 0, RET_AC,
                       lambda l: ["mh0", "mh1", "nsh", "sqm", "sdm", "sq1", "sd1", "hi1", "sqf", "sdf"] + [f"o{b}" for b in range(NBLK)] * (l == DEPTH - 1))


def build(nc, io, outs, scratch):
    START, FREED_BY, KT = number_jobs()
    TILES = len(FREED_BY)
    PEV, VEV, ACV = marks_pe(), marks_ve(), marks_ac()

    def freed(g, by):
        return FREED_BY[:g].count(by)

    with ExitStack() as ctx:
        def sb(name, cols, dt=F32):
            return ctx.enter_context(nc.sbuf_tensor(name, [128, cols], dt))

        def sem(name):
            return ctx.enter_context(nc.semaphore(name))

        h_hi, h_lo = sb("h_hi", KD * TOK, F32R), sb("h_lo", KD * TOK, F32R)
        r_hi, r_lo = sb("r_hi", 4 * TOK, F32R), sb("r_lo", 4 * TOK, F32R)
        w_raw, w_hi, w_lo = sb("w_raw", 2 * D), sb("w_hi", 2 * D, F32R), sb("w_lo", 2 * D, F32R)
        c1 = sb("c1", NC1)
        par = sb("par", 162)
        mod = sb("mod", 48 * NSTREAM)
        mulp = sb("mulp", 4 * 8 * NSTREAM)
        nsh = sb("nsh", A_T * NSTREAM)
        psh = sb("psh", A_T * DEC_B)
        lw = sb("lw", 2 * D)
        acc = sb("acc", KD * TOK)
        scr = sb("scr", SCR)
        ps = ctx.enter_context(nc.psum_tensor("ps", [128, 8, 512], F32))

        def tiles(buf, n=TOK):
            return buf[:].rearrange("p (t n) -> p t n", n=n)

        H = (tiles(h_hi), tiles(h_lo))
        R = (tiles(r_hi), tiles(r_lo))
        WR, WH, WL = (b[:].rearrange("p (s k n) -> p s k n", s=2, n=128) for b in (w_raw, w_hi, w_lo))
        ACC = tiles(acc)
        ident, bones, ones = c1[:, C_ID:C_ID + 128], c1[:, C_BD:C_BD + 128], c1[:, C_ONE:C_ONE + 128]
        MOD = mod[:].rearrange("p (t s) -> p t s", s=NSTREAM)
        MUL = mulp[:].rearrange("p (w t s) -> p w t s", w=4, s=NSTREAM)
        NSH = nsh[:].rearrange("p (t s) -> p t s", s=NSTREAM)
        PSH = psh[:].rearrange("p (t s) -> p t s", s=DEC_B)
        P_ADA, P_PRE, P_POST, P_MU = 0, 48, 64, 80
        P_W0, P_A0, P_KK, P_KA, P_RK, P_LW, P_LB = (106 + 8 * i for i in range(7))

        def cut(at, cols, n=None):
            v = scr[:, at:at + cols]
            return (v.rearrange("p (t n) -> p t n", n=n) if n else v), at + cols

        X, at = cut(0, KD * TOK, TOK)
        S1, at = cut(at, KD * TOK, TOK)
        AW, _ = cut(at, 2 * 4096)
        XR, at2 = cut(at, NBLK * D, D)
        TM, at3 = cut(at, 2 * TOK, TOK)
        FT, at3 = cut(at3, 2 * TOK, TOK)
        RS, at3 = cut(at3, TOK)
        at4 = 2 * KD * TOK + 8192
        PR, at4 = cut(at4, 256)
        CR, at4 = cut(at4, D)
        CT, at4 = cut(at4, 8 * NSTREAM, NSTREAM)

        ZL, at = cut(0, 2 * TOK, TOK)
        RKVZ, at = cut(at, 3 * TOK, TOK)
        r_b, k_b, v_b = RKVZ[:, 0], RKVZ[:, 1], RKVZ[:, 2]
        ic, at = cut(at, TOK)
        kk, at = cut(at, TOK)
        bo, at = cut(at, TOK)
        cu, at = cut(at, TOK)
        lam, at = cut(at, TOK)
        t1, at = cut(at, TOK)
        gt = lam
        RM, _ = cut(at - 2 * TOK, 1024, 128)
        x_at = at
        ATR, at = cut(at, NBLK * 512, 512)
        XM, _ = cut(x_at, 2 * NBLK * 128, 128)
        XTM, _ = cut(x_at + 2 * NBLK * 128, 2 * NBLK * 128, 128)
        BKM, _ = cut(x_at, 2048, 128)
        lt_at = at
        LTI, at = cut(at, 2 * NBLK * 128, 128)
        TNS, _ = cut(lt_at, 1024, 128)
        WM, _ = cut(lt_at, 1024, 128)
        ak_at = at
        AKT, at = cut(at, 2 * NBLK * 128, 128)
        STS, _ = cut(ak_at, 1024, 128)
        BRT, at = cut(at, 2 * NBLK * 128, 128)
        KRT, at = cut(at, 2 * NBLK * 128, 128)
        TOKB, at = cut(at, NBLK * 512, 128)
        S, at = cut(at, 128)
        SS, at = cut(at, 128)
        TN, at = cut(at, 128)
        PC, at = cut(at, PB + DEC_B)
        MID, at = cut(at, PB)
        EM, at = cut(at, PB)
        SN, at = cut(at, 1024, 128)
        SPO, at = cut(at, 128)
        ZT, at = cut(at, 2 * TOK, TOK)
        assert at <= SCR, at
        Z_, U0, WT, U = (b.rearrange("p (t n) -> p t n", n=128) for b in (k_b, ic, kk, v_b))
        yb = cu
        T1 = AKT

        QKV, at = cut(0, 8 * TOK, TOK)
        Y4 = QKV[:, 4:8]
        QX = scr[:, 0:2048].rearrange("p (k b n) -> p k b n", k=2, n=128)
        SG, at = cut(at, 4 * TOK, TOK)
        VT, at = cut(at, NBLK * 512, 512)
        KP, at = cut(at, NBLK * 256, 256)
        PT, at = cut(at, 1280 + 128)
        QD, at = cut(at, 256, 128)
        SR, at = cut(at, 3 * 1024, 1024)
        RT1, at = cut(at, 2 * TOK, TOK)
        C2, at = cut(at, 2 * TOK + 780)
        assert at <= SCR, at
        KS = lw[:].rearrange("p (b k n) -> p b k n", b=DEC_B, n=128)
        H_MW, H_MS, H_QD = (C2[:, 2 * TOK + a:2 * TOK + a + n] for a, n in ((0, 512), (512, 128), (640, 128)))
        H_KP, H_KS = C2[:, 2 * TOK + 768:2 * TOK + 772], C2[:, 2 * TOK + 772:2 * TOK + 780]
        cosT, sinT = C2[:, 0:TOK], C2[:, TOK:2 * TOK]
        NSR, _ = cut(2 * KD * TOK + 3200, A_COLS)
        SHR, _ = cut(KD * TOK, A_COLS)
        MS, _ = cut(2 * KD * TOK + 3200, KD * TOK, TOK)

        pe_mark, ve_mark, ac_mark = sem("pe_mark"), sem("ve_mark"), sem("ac_mark")
        ve_order, ac_order = sem("ve_order"), sem("ac_order")
        w_in = [sem("w_in0"), sem("w_in1")]
        hi_done, lo_done, mm_done = sem("hi_done"), sem("lo_done"), sem("mm_done")
        psum_read_a, psum_read_v = sem("psum_read_a"), sem("psum_read_v")
        tmp_used, relu_done, sq_done, up_sq = sem("tmp_used"), sem("relu_done"), sem("sq_done"), sem("up_sq")
        const_in, par_in, ada_in, x_in, ret_in, rw_in, lw_in, m_in = (
            sem("const_in"), sem("par_in"), [sem("ada_in0"), sem("ada_in1")], sem("x_in"), sem("ret_in"), sem("rw_in"),
            sem("lw_in"), sem("m_in"))
        sr_in = [sem(f"sr_in{i}") for i in range(3)]
        sr_out = [sem(f"sr_out{i}") for i in range(3)]
        ada_used, ada_row, ada_turned = sem("ada_used"), sem("ada_row"), sem("ada_turned")
        z_out, z_in = [sem("z_out0"), sem("z_out1")], sem("z_in")
        x_out, m_out, rw_out, sh_out, y_out, kp_out = (
            sem("x_out"), sem("m_out"), sem("rw_out"), sem("sh_out"), sem("y_out"), sem("kp_out"))
        zero_done = sem("zero_done")

        def halves(a):
            return a.rearrange("p (h n) -> p h n", h=2)

        def two_banks(b):
            return ps[:, b:b + 2, 0:HALF]

        w_in_v = io["w_in"].rearrange("l (k p) (c n) -> l c p k n", p=128, n=128)
        up_v = io["w_ffn_up"].rearrange("l (k p) (c n) -> l c p k n", p=128, n=128)
        down_v = io["w_ffn_down"].rearrange("l (f k p) (c n) -> l f c p k n", p=128, k=4, n=128)
        ba_v = io["w_branch_a"].rearrange("l (f k p) (c n) -> l f c p k n", p=128, k=4, n=128)
        bb_v = io["w_branch_b"].rearrange("l (f k p) (c n) -> l f c p k n", p=128, k=4, n=128)
        out_v = io["w_out"].rearrange("l (f k p) (c n) -> l f c p k n", p=128, k=4, n=128)
        ada_v = io["ada_w"].rearrange("l (k p) (c n) -> l c p k n", p=128, n=512)

        def weight_of(l, name, i):
            if name == "lora":
                return w_in_v[l, 24 + i]
            if name.startswith("rkv"):
                return w_in_v[l, int(name[3:]) + 8 * i]
            if name.startswith("gate"):
                return w_in_v[l, 74 + 8 * int(name[4:]) + i]
            if name.startswith("z"):
                h, i = divmod(Z_TILES * int(name[1:]) + i, 12)
                base = 26 + 2 * h + i if i < 2 else 34 + 2 * h + i - 2 if i < 4 else 42 + 4 * h + i - 4 if i < 8 else 58 + 4 * h + i - 8
                return w_in_v[l, base]
            if name.startswith("up"):
                return up_v[l, 4 * int(name[2:]) + i]
            v = {"ba": ba_v, "bb": bb_v, "ou": out_v, "do": down_v}[name[:2]]
            return v[l, int(name[-1])][i]

        def job_tiles(eng, l, name, tile, peel=0):
            g0 = START[l, name]
            n = dict((j[0], j[1]) for j in jobs_of_layer())[name]
            if n < 8 or n == 12:
                for i in range(n):
                    tile(g0 + i, i, (g0 + i) % 2)
                return
            for i in range(peel):
                tile(g0 + i, i, (g0 + i) % 2)
            with eng.Fori(peel // 2, n // 2) as turn:
                for s in range(2):
                    tile(turn * 2 + (g0 + s), turn * 2 + s, (g0 + s) % 2)

        def part_of(l, p, emit):
            n, at_ = 4 * len(filler(l, p)), [0]
            quarters = dict(POINTS)

            def point(name):
                for _ in range(min(quarters[name], n - at_[0])):
                    emit(at_[0] // 4, at_[0] % 4)
                    at_[0] += 1
            return point

        block = ctx.enter_context(nc.Block())

        def wait_mark(eng, which, *key):
            s_, v_ = {"pe": (pe_mark, PEV), "ve": (ve_mark, VEV), "ac": (ac_mark, ACV)}[which]
            eng.wait_ge(s_, v_[key])

        @block.sync
        def _(sp):
            def load_tile(l, name):
                kt = dict((j[0], j[2]) for j in jobs_of_layer())[name]

                def tile(g, i, s):
                    if isinstance(g, int) and g - 4 in spilled:
                        f, place = spilled[g - 4]
                        sp.wait_ge(psum_read_a, freed(g - 3, "a"))
                        sp.dma_start(scratch["z"][place], ZT[:, f % 2]).then_inc(z_out[f % 2], 16)
                    if not isinstance(g, int) or g >= 2:
                        sp.wait_ge(lo_done, g - 1)
                    sp.dma_start(WR[:, s, 0:kt], weight_of(l, name, i)).then_inc(w_in[s], 16)
                job_tiles(sp, l, name, tile, 4 if name[:2] == "ba" else 2)

            spilled = {}
            for l in range(DEPTH):
                for p in range(PAIRS):
                    for i, (g, place, _) in enumerate(filler(l, p)):
                        spilled[g] = (spill_number(l, p, i), place)
            sp.dma_start(c1[:], io["const1"]).then_inc(const_in, 16)
            for l in range(DEPTH):
                load_tile(l, "lora")
                wait_mark(sp, "pe", l, "x4" if l == 0 else "ct")
                for n in range(12):
                    m = 12 * l + n
                    if m >= 2:
                        sp.wait_ge(ada_used, m - 1)
                    sp.dma_start(AW[:, 4096 * (n % 2):4096 * (n % 2) + 4096].rearrange("p (k n) -> p k n", k=8), ada_v[l, n]
                                 ).then_inc(ada_in[n % 2], 16)
                for name, *_ in jobs_of_layer()[1:]:
                    load_tile(l, name)

        @block.gpsimd
        def _(po):
            for l in range(DEPTH):
                if l:
                    wait_mark(po, "ve", l - 1, "x2")
                    wait_mark(po, "pe", l - 1, "ffn")
                    po.wait_ge(sh_out, 32 * l)
                rows = [(0, "ada_b", 0), (48, "norm_pre", 0), (64, "norm_post", 0), (80, "a_mu", 0)]
                rows += [(8 * j, nm, 128) for j, nm in enumerate(["a_w0", "a_a0", "a_kk", "a_ka", "a_rk", "a_ln_w", "a_ln_b"])]
                for r0, nm, col in rows:
                    src = io[nm][l]
                    src = src.rearrange("a b -> (a b)") if len(src.shape) == 2 else src
                    n = src.shape[0] // 128
                    po.dma_start(PR[r0:r0 + n, col:col + 128], src.rearrange("(t n) -> t n", n=128)).then_inc(par_in, 16)
                po.dma_start(CR[0:1, :], io["c_prompt"]).then_inc(par_in, 16)
                po.dma_start(CR[1:NSTREAM, :], io["c_sample"]).then_inc(par_in, 16)
                po.dma_start(SHR[0:DEC_B, :], io["state_shift"][l]).then_inc(par_in, 16)
                if l == 0:
                    po.dma_start(XR[:, 0:PB], io["x_prompt"][0].rearrange("(b p) n -> p b n", p=128)).then_inc(x_in, 16)
                    po.dma_start(XR[:, PB], io["x_sample"].rearrange("b t n -> (b t) n")).then_inc(x_in, 16)
                po.dma_start(lw[0:64, 0:D], io["a_w2"][l]).then_inc(lw_in, 16)
                po.dma_start(lw[64:128, 0:D], io["a_a2"][l]).then_inc(lw_in, 16)
                po.dma_start(lw[:, D:2 * D], io["a_g2"][l]).then_inc(lw_in, 16)
                if l == 0:
                    wait_mark(po, "ac", 0, "x4")
                po.dma_start(scratch["x"], X).then_inc(x_out, 16)
                wait_mark(po, "ve", l, "h0")
                po.wait_ge(x_out, 16 * (l + 1))
                po.memset(SN, 0.0).then_inc(zero_done, 1)
                po.wait_ge(zero_done, l + 1)
                for p in range(PAIRS):
                    n = 8 * l + p
                    if p:
                        for i in range(3):
                            f = spill_number(l, p - 1, Z_TILES + i)
                            po.wait_ge(z_out[f % 2], 16 * (f // 2 + 1))
                        po.dma_start(RKVZ, scratch["z"][PAIRS * Z_TILES + 3 * (p - 1):PAIRS * Z_TILES + 3 * p].rearrange("t p n -> p t n")
                                     ).then_inc(z_in, 16)
                        po.wait_ge(rw_out, 64 * n)
                    for q in range(2):
                        sl = slice(64 * q, 64 * q + 64)
                        po.dma_start(SN[sl, :, sl], io["state_rwkv"][l, :, 2 * p + q].rearrange("b v k -> v b k")).then_inc(rw_in, 16)
                    wait_mark(po, "ac", l, "rw", p, "sout")
                    for q in range(2):
                        sl = slice(64 * q, 64 * q + 64)
                        po.dma_start(outs[6][l, :, 2 * p + q].rearrange("b v k -> v b k"), SN[sl, :, sl]).then_inc(rw_out, 16)
                        po.dma_start(outs[3][l, 0, 2 * p + q], SPO[sl, sl]).then_inc(rw_out, 16)
                po.wait_ge(tmp_used, 48 * l + 8)
                po.dma_start(scratch["m"], ACC).then_inc(m_out, 16)
                po.wait_ge(rw_out, 64 * 8 * (l + 1))
                po.dma_start(C2[:, 0:2 * TOK], io["const2"][:, 0:2 * TOK]).then_inc(ret_in, 16)
                for h in range(RH):
                    if h:
                        wait_mark(po, "ve", l, "rt", h - 1, "split")
                    else:
                        wait_mark(po, "ve", l, "rw", PAIRS - 1, "split")
                        for i in range(Z_TILES):
                            f = spill_number(l, PAIRS - 1, i)
                            po.wait_ge(z_out[f % 2], 16 * (f // 2 + 1))
                    po.dma_start(QKV, scratch["z"][12 * h:12 * h + 8].rearrange("t p n -> p t n")).then_inc(z_in, 16)
                    po.dma_start(SG, scratch["z"][12 * h + 8:12 * h + 12].rearrange("t p n -> p t n")).then_inc(z_in, 16)
                    for a, n, src in ((0, 512, K_MW + 512 * h), (512, 128, K_MS + 128 * h), (640, 128, K_QD + 128 * h),
                                      (768, 4, K_KP + 4 * h), (772, 8, K_KS + 8 * h)):
                        po.dma_start(C2[:, 2 * TOK + a:2 * TOK + a + n], io["const2"][:, src:src + n]).then_inc(ret_in, 16)
                    for b in range(DEC_B + 1):
                        n = 8 * (RH * l + h) + b
                        if b < DEC_B:
                            if n >= 3:
                                po.wait_ge(sr_out[n % 3], 16 * (n // 3))
                            po.dma_start(SR[:, n % 3].rearrange("p (k v) -> p k v", k=2),
                                         io["state_ret"][l, b, h].rearrange("(k p) v -> p k v", p=128)).then_inc(sr_in[n % 3], 16)
                        if b >= 1:
                            wait_mark(po, "ve", l, "rt", h, f"ss{b - 1}")
                            po.dma_start(outs[7][l, b - 1, h].rearrange("(k p) v -> p k v", p=128),
                                         SR[:, (n - 1) % 3].rearrange("p (k v) -> p k v", k=2)).then_inc(sr_out[(n - 1) % 3], 16)
                    wait_mark(po, "ac", l, "rt", h, "sp")
                    po.dma_start(outs[4][l, 0, h].rearrange("(k p) v -> p k v", p=128), RT1[:, :, 0:512]).then_inc(kp_out, 16)
                wait_mark(po, "ve", l, "rt", RH - 1, "split")
                po.wait_ge(kp_out, 16 * RH * (l + 1))
                for i in range(3):
                    po.wait_ge(sr_out[i], 16 * ((32 * (l + 1) - i + 2) // 3))
                po.wait_ge(m_out, 16 * (l + 1))
                po.dma_start(MS, scratch["m"]).then_inc(m_in, 16)
                po.dma_start(X, scratch["x"]).then_inc(m_in, 16)
                wait_mark(po, "ac", l, "nsh")
                po.dma_start(outs[2][l], NSR[0:1, :]).then_inc(sh_out, 16)
                po.dma_start(outs[5][l], NSR[1:NSTREAM, :]).then_inc(sh_out, 16)
            for b in range(NBLK):
                wait_mark(po, "ac", DEPTH - 1, f"o{b}")
                dst = outs[0][0, 128 * b:128 * b + 128] if b < PB else outs[1].rearrange("b t n -> (b t) n")
                po.dma_start(dst, XR[:, b]).then_inc(y_out, 16)
            po.wait_ge(y_out, 16 * NBLK)
            po.wait_ge(sh_out, 32 * DEPTH)

        @block.tensor
        def _(pe):
            mark_n = [0]

            def mark(ins, *key):
                mark_n[0] += 1
                assert PEV[key] == mark_n[0], (key, mark_n)
                ins.then_inc(pe_mark, 1)

            def mm(out, lhsT, rhs, start=True, stop=True):
                return pe.matmul(out, lhsT, rhs, start=start, stop=stop, skip_group_check=True)

            def tr(out, in_):
                n = in_.shape[0]
                return pe.transpose(out, in_, c1[0:n, C_ID:C_ID + n])

            def gemm(l, name):
                g0 = START[l, name]
                kt = dict((j[0], j[2]) for j in jobs_of_layer())[name]
                by = FREED_BY[g0]
                hi, lo = R if kt == 4 else H
                pe.wait_ge(psum_read_a, freed(g0, "a"))
                if freed(g0, "v"):
                    pe.wait_ge(psum_read_v, freed(g0, "v"))

                def tile(g, i, s):
                    pe.wait_ge(lo_done, g + 1)
                    if not isinstance(i, int) or i >= 2:
                        pe.wait_ge(psum_read_a if by == "a" else psum_read_v, i + (freed(g0, by) - 1))
                    for k in range(kt):
                        for n_, (w, x) in enumerate(((WH, hi), (WH, lo), (WL, hi))):
                            for hf in range(2):
                                last = mm(ps[:, 2 * s + hf, 0:HALF], w[:, s, k], x[:, k, HALF * hf:HALF * hf + HALF],
                                          start=(k == 0 and n_ == 0), stop=(k == kt - 1 and n_ == 2))
                    last.then_inc(mm_done, 1)
                job_tiles(pe, l, name, tile, 2)

            def psum_clear(g):
                pe.wait_ge(psum_read_a, freed(g, "a"))
                if freed(g, "v"):
                    pe.wait_ge(psum_read_v, freed(g, "v"))

            def channel_sums(mat, src, n, bank):
                for hf in range(2):
                    for i in range(n):
                        last = mm(ps[:, bank + hf, 0:HALF], mat, src[:, i, HALF * hf:HALF * hf + HALF], i == 0, i == n - 1)
                return last

            def rwkv(l, p):
                W = lambda e, n: wait_mark(pe, e, l, "rw", p, n)
                M = lambda ins, n: mark(ins, l, "rw", p, n)
                tiles_ = filler(l, p)

                def quarter(i, q):
                    g = tiles_[i][0]
                    if q == 0:
                        pe.wait_ge(lo_done, g + 1)
                        psum_clear(g)
                    for k in (2 * q, 2 * q + 1):
                        for n_, (w, x) in enumerate(((WH, H[0]), (WH, H[1]), (WL, H[0]))):
                            for hf in range(2):
                                last = mm(ps[:, hf, 0:HALF], w[:, g % 2, k], x[:, k, HALF * hf:HALF * hf + HALF],
                                          start=(k == 0 and n_ == 0), stop=(k == 7 and n_ == 2))
                    if q == 3:
                        last.then_inc(mm_done, 1)
                point = part_of(l, p, quarter)
                if p % 4 == 0:
                    psum_clear(START[l, f"z{p}"])
                else:
                    wait_mark(pe, "ve", l, "rw", p - 1, "var")
                ch = slice(128 * p, 128 * p + 128)
                for hf in range(2):
                    mm(ps[:, 2 + hf, 0:HALF], lw[0:64, ch], ZL[0:64, 0, HALF * hf:HALF * hf + HALF])
                for hf in range(2):
                    last = mm(ps[:, 4 + hf, 0:HALF], lw[64:128, ch], ZL[64:128, 0, HALF * hf:HALF * hf + HALF])
                M(last, "wi")
                point("sq")
                W("ve", "sq")
                if p % 4:
                    wait_mark(pe, "ac", l, "rw", p - 1, "gate")
                M(channel_sums(bones, t1[:, None, :], 1, 6), "ss")
                point("rk")
                W("ve", "rk")
                W("ac", "sig")
                M(channel_sums(bones, t1[:, None, :], 1, 2), "bs")
                point("ab")
                W("ve", "abkr")
                W("ac", "nr")
                for b in range(NBLK):
                    if b == 4:
                        W("ac", "t0")
                    for j, src in enumerate((kk, ic, k_b, v_b)):
                        last = tr(ps[:, b % 4 + 4, 128 * j:128 * j + 128], src[:, 128 * b:128 * b + 128])
                    M(last, f"t{b}")
                for j in range(2 * NBLK):
                    b, w = j // 2, (ic, k_b)[j % 2]
                    if j >= 4:
                        W("ve", f"s{j - 4}")
                    elif j >= 2:
                        W("ac", f"t{j}")
                    M(mm(ps[:, (2, 3, 6, 7)[j % 4], :], w[:, 128 * b:128 * b + 128], ATR[:, b]), f"s{j}")
                W("ac", f"t{NBLK - 1}")
                point("z")
                W("ve", f"s{2 * NBLK - 1}")

                def flat(bank, c, n):
                    return ps[:, bank + c // 512, c % 512:c % 512 + n]
                for m in range(2 * NBLK):
                    last = mm(flat(5, 128 * m, 128), AKT[:, m], TOKB[:, 4 * (m // 2) + 3])
                M(last, "z")
                point("lti")
                W("ve", "lti")
                for g in range(3):
                    for m in range(4 * g, min(4 * g + 4, 2 * NBLK)):
                        last = tr(ps[:, 2 + g, 128 * (m % 4):128 * (m % 4) + 128], LTI[:, m])
                    M(last, f"lt{g}")
                W("ac", "z")
                tb, xb_ = (2, 3, 4), (5, 6, 7)
                for lv in range(1, LEVELS):
                    for g in rw_groups(lv):
                        if lv == 1:
                            W("ve", f"x0.{g}")
                        else:
                            W("ac", f"XT{lv - 1}.{g}")
                        for m in range(4 * g, min(4 * g + 4, 2 * NBLK)):
                            last = mm(ps[:, tb[g], 128 * (m % 4):128 * (m % 4) + 128], LTI[:, m], XM[:, m])
                        M(last, f"T{lv}.{g}")
                    point(f"la{lv}")
                    for g in rw_groups(lv):
                        W("ve", f"T{lv}.{g}")
                        for m in range(4 * g, min(4 * g + 4, 2 * NBLK)):
                            last = mm(ps[:, xb_[g], 128 * (m % 4):128 * (m % 4) + 128], XTM[:, m], T1[:, m])
                        M(last, f"X{lv}.{g}")
                        for m in range(4 * g, min(4 * g + 4, 2 * NBLK)):
                            last = mm(ps[:, tb[g], 128 * (m % 4):128 * (m % 4) + 128], T1[:, m], XTM[:, m])
                        M(last, f"XT{lv}.{g}")
                    point(f"lb{lv}")
                W("ac", f"XT{S_LEVELS - 1}.2")
                for g in (0, 1):
                    W("ac", f"XT{LEVELS - 1}.{g}")
                for m in range(2 * NBLK):
                    b, q = m // 2, m % 2
                    mm(flat(2, 128 * m, 128), XTM[:, m], Z_[:, b])
                    last = mm(flat(5, 128 * b, 128)[64 * q:64 * q + 64], TOKB[:, 4 * b, 64 * q:64 * q + 64], XTM[:, m])
                M(last, "uw")
                point("uw")
                pe.wait_ge(rw_in, 32 * (8 * l + p + 1))
                W("ac", "uw")
                for b in range(DEC_B):
                    last = tr(flat(2, 128 * b, 128), SN[:, b])
                M(last, "sT")

                def own_terms(bank, c0, b, first):
                    for q in range(2):
                        sl, o = slice(64 * q, 64 * q + 64), ps[64 * q:64 * q + 64, bank, c0:c0 + 128]
                        mm(o, U[:, b, sl], BRT[:, 2 * b + q], first, False)
                        last = mm(o, TOKB[:, 4 * b + 3, sl], KRT[:, 2 * b + q], False, True)
                    return last

                for c in range(PB):
                    t = slice(128 * c, 128 * c + 128)
                    if c:
                        W("ve", f"ss{c}")
                        M(mm(ps[:, 4, 0:128], WT[:, c], SS), f"u{c}")
                        mm(ps[:, 6, t], SS, r_b[:, t], True, False)
                    point(f"ca{c}")
                    W("ve", f"u{c}")
                    mm(ps[:, 5, 0:128], TOKB[:, 4 * c + 1], U[:, c], True, False)
                    M(mm(ps[:, 5, 0:128], TOKB[:, 4 * c + 2], TOKB[:, 4 * c + 3], False, True), f"new{c}")
                    own_terms(6, 128 * c, c, c == 0)
                    point(f"cb{c}")
                W("ve", f"new{PB - 1}")
                M(tr(ps[:, 4, 128:256], S), "spo")
                W("ac", "sT")
                W("ve", "smask")
                for b in range(DEC_B):
                    last = mm(ps[:, 5, 128:256], WM[:, b], STS[:, b], b == 0, b == DEC_B - 1)
                M(last, "su")
                for b in range(DEC_B):
                    mm(ps[:, 7, 0:128], STS[:, b], RM[:, b], b == 0, False)
                point("su")
                W("ve", "su")
                M(own_terms(7, 0, PB, False), "y")
                for b in range(DEC_B):
                    mm(flat(2, 128 * b, 128), BKM[:, b], U[:, PB], True, False)
                    last = mm(flat(2, 128 * b, 128), BKM[:, 8 + b], TOKB[:, 4 * PB + 3], False, True)
                M(last, "snew")
                point("sn")
                W("ve", "snew")
                W("ac", "spo")
                for b in range(DEC_B):
                    last = tr(flat(4, 128 * b, 128), TNS[:, b])
                M(last, "sout")
                W("ac", "y")
                M(channel_sums(bones, yb[:, None, :], 1, 2), "gn1")
                for hf in range(2):
                    last = mm(ps[:, 6 + hf, 0:HALF], lw[:, D + 128 * p:D + 128 * p + 128], ZL[:, 1, HALF * hf:HALF * hf + HALF])
                M(last, "gate")
                point("so")
                W("ve", "yc")
                W("ac", "sout")
                M(channel_sums(bones, t1[:, None, :], 1, 4), "gn2")
                point("gn")
                point("end")

            def retention(l, h):
                W = lambda e, n: wait_mark(pe, e, l, "rt", h, n)
                M = lambda ins, n: mark(ins, l, "rt", h, n)
                psum_clear(START[l, f"bb{h}"])
                W("ve", "rope")
                for b in range(NBLK):
                    t = slice(128 * b, 128 * b + 128)
                    for j in range(4):
                        tr(ps[:, b, 128 * j:128 * j + 128], QKV[:, 4 + j, t])
                    for j in range(2):
                        last = tr(ps[:, 5 + b // 2, 256 * (b % 2) + 128 * j:256 * (b % 2) + 128 * j + 128], QKV[:, 2 + j, t])
                M(last, "tr")
                W("ac", "vk")
                for b in range(NBLK):
                    n = SEQ - 128 * b if b < PB else 128
                    for j in range(2):
                        last = mm(ps[:, b, 0:n], QKV[:, 2 + j, 128 * b:128 * b + 128], QKV[:, j, 128 * b:128 * b + n], j == 0, j == 1)
                    M(last, f"s{b}")
                for k in range(2):
                    for b in range(PB):
                        last = mm(ps[:, 5 + k, :], KP[:, b, 128 * k:128 * k + 128], VT[:, b], b == 0, b == PB - 1)
                M(last, "sp")
                for b in range(NBLK):
                    W("ve", f"p{b}")
                for v in range(4):
                    at_ = 0
                    for b in range(PB):
                        n = SEQ - 128 * b
                        mm(ps[:, v, 128 * b:512], VT[:, b, 128 * v:128 * v + 128], PT[:, at_:at_ + n], b == 0, b == PB - 1)
                        at_ += n
                for v in range(4):
                    mm(ps[:, 4, 128 * v:128 * v + 128], VT[:, PB, 128 * v:128 * v + 128], PT[:, 1280:1408], v == 0, False)
                W("ve", "ks")
                W("ve", "qx")
                W("ac", "sp")
                for b in range(DEC_B):
                    n = 8 * (RH * l + h) + b
                    pe.wait_ge(sr_in[n % 3], 16 * (n // 3 + 1))
                    for v in range(4):
                        for k in range(2):
                            c = 512 * k + 128 * v
                            mm(ps[:, 4, 128 * v:128 * v + 128], SR[:, n % 3, c:c + 128], QX[:, k, b], False, b == DEC_B - 1 and k == 1)
                    if b:
                        W("ve", f"ss{b - 1}")
                    for k in range(2):
                        last = mm(ps[:, 5 + k, :], KS[:, b, k], VT[:, PB])
                    M(last, f"ss{b}")
                W("ac", "ysq")
                M(channel_sums(ones, VT.rearrange("p a b -> p (a b)").rearrange("p (t n) -> p t n", n=TOK), 4, 0), "rn")

            def norm_sums(l, name, wait, src):
                wait_mark(pe, "ac", l, wait)
                mark(channel_sums(ones, src, KD, 0), l, name)

            pe.wait_ge(const_in, 16)
            for l in range(DEPTH):
                pe.wait_ge(par_in, 14 * 16 * (l + 1))
                if l:
                    wait_mark(pe, "ve", l - 1, "varf")
                tr(ps[:, 0, 0:106], PR[0:106, 0:128])
                tr(ps[:, 0, 106:162], PR[0:56, 128:256])
                for t in range(A_T):
                    last = tr(ps[:, 1, 8 * t:8 * t + 8], SHR[0:DEC_B, 128 * t:128 * t + 128])
                mark(last, l, "par")
                wait_mark(pe, "ac", l, "silu")
                for k in range(KD):
                    last = tr(ps[:, 2, NSTREAM * k:NSTREAM * k + NSTREAM], CR[0:NSTREAM, 128 * k:128 * k + 128])
                mark(last, l, "ct")
                if l == 0:
                    pe.wait_ge(x_in, 32)
                    wait_mark(pe, "ac", l, "par")
                    wait_mark(pe, "ac", l, "ct")
                    for b in range(NBLK):
                        if b == 4:
                            wait_mark(pe, "ac", l, "x0")
                        for k in range(KD):
                            last = tr(ps[:, 2 * (b % 4) + k // 4, 128 * (k % 4):128 * (k % 4) + 128], XR[:, b, 128 * k:128 * k + 128])
                        mark(last, l, f"x{b}")
                    wait_mark(pe, "ac", l, "x4")
                wait_mark(pe, "ac", l, "par")
                wait_mark(pe, "ac", l, "ct")
                for n in range(13):
                    m = 12 * l + n
                    if n < 12:
                        pe.wait_ge(ada_in[n % 2], 16 * (6 * l + n // 2 + 1))
                        if n >= 2:
                            pe.wait_ge(ada_row, m - 1)
                        a = AW[:, 4096 * (n % 2):4096 * (n % 2) + 4096].rearrange("p (k n) -> p k n", k=8)
                        for k in range(KD):
                            last = mm(ps[0:NSTREAM, 5 + n % 2, :], CT[:, k], a[:, k], k == 0, k == KD - 1)
                        last.then_inc(ada_used, 1)
                    if n:
                        pe.wait_ge(ada_row, m)
                        for j in range(4):
                            t = 4 * (n - 1) + j
                            last = tr(ps[:, 7, NSTREAM * t:NSTREAM * t + NSTREAM], CR[0:NSTREAM, 512 * ((n - 1) % 2) + 128 * j:512 * ((n - 1) % 2) + 128 * j + 128])
                        last.then_inc(ada_turned, 1)
                norm_sums(l, "n0", "sq0", S1)
                wait_mark(pe, "ve", l, "h0")
                gemm(l, "lora")
                gemm(l, "rkv0")
                wait_mark(pe, "ac", l, "lora")
                pe.wait_ge(lw_in, 48 * (l + 1))
                for p in range(PAIRS):
                    rwkv(l, p)
                    if p % 4 == 3:
                        wait_mark(pe, "ve", l, "rw", p, "split")
                        gemm(l, f"ba{p // 4}")
                gemm(l, "gate0")
                for h in range(RH):
                    retention(l, h)
                    wait_mark(pe, "ve", l, "rt", h, "split")
                    gemm(l, f"bb{h}")
                gemm(l, "gate1")
                for j in range(2):
                    wait_mark(pe, "ve", l, f"ms{j}")
                    gemm(l, f"out{j}")
                psum_clear(START[l, "up0"])
                for t in range(A_T):
                    last = tr(ps[0:NSTREAM, t // 4, 128 * (t % 4):128 * (t % 4) + 128], NSH[:, t])
                mark(last, l, "nsh")
                wait_mark(pe, "ac", l, "nsh")
                norm_sums(l, "mix", "sqm", ACC)
                wait_mark(pe, "ve", l, "varm")
                norm_sums(l, "n1", "sq1", S1)
                wait_mark(pe, "ve", l, "h1")
                for f in range(8):
                    gemm(l, f"up{f}")
                    pe.wait_ge(tmp_used, 48 * l + 16 + 4 * (f + 1))
                    gemm(l, f"down{f}")
                psum_clear(START[l, "down7"] + 8)
                norm_sums(l, "ffn", "sqf", ACC)
            wait_mark(pe, "ve", DEPTH - 1, "x2")
            for b in range(NBLK):
                if b == 4:
                    wait_mark(pe, "ac", DEPTH - 1, "o0")
                for k in range(KD):
                    last = tr(ps[:, 2 * (b % 4) + k // 4, 128 * (k % 4):128 * (k % 4) + 128], X[:, k, 128 * b:128 * b + 128])
                mark(last, DEPTH - 1, f"o{b}")

        @block.scalar
        def _(ac):
            mark_n, order_n = [0], [0]

            def do(out, in_, f=ACT.Copy, **kw):
                order_n[0] += 1
                ac.activation(out, in_, f, **kw).then_inc(ac_order, 1)
                ac.wait_ge(ac_order, order_n[0])

            def mark(*key):
                mark_n[0] += 1
                assert ACV[key] == mark_n[0], (key, mark_n)
                ac.sem_inc(ac_mark, 1)

            def split(g, s, kt):
                ac.wait_ge(w_in[s], (g - s) * 8 + 16)
                if not isinstance(g, int) or g >= 2:
                    ac.wait_ge(mm_done, g - 1)
                ac.activation(WH[:, s, 0:kt], WR[:, s, 0:kt], ACT.Copy).then_inc(hi_done, 1)

            def gemm(l, name):
                g0, n, kt = START[l, name], *next((j[1], j[2]) for j in jobs_of_layer() if j[0] == name)
                t0 = 48 * l + (8 if name == "gate1" else 16 + 4 * int(name[2:]) if name[:2] == "up" else 0)

                def tile(g, i, s):
                    par_ = i % 2 if isinstance(i, int) else (s - g0) % 2
                    if FREED_BY[g0] == "a":
                        ac.wait_ge(mm_done, g + 1)
                        src = two_banks(2 * s)
                        if name == "lora":
                            ac.activation(halves(ZL[:, i]), src, ACT.Copy).then_inc(psum_read_a, 1)
                        elif name.startswith("rkv"):
                            ac.activation(halves(RKVZ[:, i]), src, ACT.Copy).then_inc(psum_read_a, 1)
                        elif name.startswith("gate"):
                            if not isinstance(i, int) or i + t0 >= 2:
                                ac.wait_ge(tmp_used, i + (t0 - 1))
                            ac.activation(halves(TM[:, par_]), src, ACT.Sigmoid).then_inc(psum_read_a, 1)
                        else:
                            ac.wait_ge(tmp_used, i + (t0 - 1))
                            ac.activation(halves(TM[:, par_]), src, ACT.Relu).then_inc(psum_read_a, 1)
                            ac.wait_ge(psum_read_a, freed(g, "a") + 1)
                            ac.activation(R[0][:, i], TM[:, par_], ACT.Square).then_inc(up_sq, 1)
                job_tail(l, name, tile)

            def job_tail(l, name, tile):
                g0 = START[l, name]

                def both(g, i, s):
                    tile(g, i, s)
                    split_next(g, s)
                job_tiles_ve(ac, l, name, both)

            def split_next(g, s):
                if isinstance(g, int):
                    if g + 2 < TILES:
                        split(g + 2, s, KT[g + 2])
                else:
                    split(g + 2, s, cur_kt[0])

            cur_kt = [0]

            def job_tiles_ve(eng, l, name, tile):
                g0 = START[l, name]
                n, kt = next((j[1], j[2]) for j in jobs_of_layer() if j[0] == name)
                if n != 8:
                    for i in range(n):
                        tile(g0 + i, i, (g0 + i) % 2)
                    return
                cur_kt[0] = kt
                for i in range(2):
                    tile(g0 + i, i, (g0 + i) % 2)
                with eng.Fori(1, n // 2 - 1) as turn:
                    for s in range(2):
                        tile(turn * 2 + (g0 + s), turn * 2 + s, (g0 + s) % 2)
                for i in range(n - 2, n):
                    tile(g0 + i, i, (g0 + i) % 2)

            def norm(l, src, sq, tag):
                do(sq, src, ACT.Square)
                mark(l, "sq" + tag)
                wait_mark(ac, "ve", l, "var" + tag)
                do(RS, RS, ACT.Sqrt)
                mark(l, "sd" + tag)

            def high_part(l, tag, g):
                wait_mark(ac, "ve", l, "hx" + tag)
                if g:
                    ac.wait_ge(mm_done, g)
                do(H[0], S1)
                mark(l, "hi" + tag)

            def rwkv(l, p):
                W = lambda e, n: wait_mark(ac, e, l, "rw", p, n)
                M = lambda n: mark(l, "rw", p, n)
                col = lambda c: par[:, c + p:c + p + 1]
                tiles_ = filler(l, p)

                def beside(i, q):
                    if q == 3:
                        g, _, gate = tiles_[i]
                        f = spill_number(l, p, i)
                        if f >= 2:
                            ac.wait_ge(z_out[f % 2], 16 * (f // 2))
                        ac.wait_ge(mm_done, g + 1)
                        ac.activation(halves(ZT[:, f % 2]), two_banks(0), ACT.Silu if gate else ACT.Copy).then_inc(psum_read_a, 1)
                        split_next(g, g % 2)
                point = part_of(l, p, beside)
                W("pe", "wi")
                do(halves(lam), two_banks(2), ACT.Sigmoid, bias=col(P_W0))
                do(halves(ic), two_banks(4), ACT.Sigmoid, bias=col(P_A0))
                M("sig")
                point("sq")
                W("pe", "ss")
                do(halves(t1), two_banks(6), ACT.Sqrt)
                M("nr")
                point("rk")
                W("ve", "ea")
                do(t1, t1, ACT.Exp)
                M("ea")
                do(lam, cu, ACT.Exp, scale=-1.0)
                do(EM, MID, ACT.Exp)
                do(cu, cu, ACT.Exp)
                M("exp")
                point("ab")
                for b in range(NBLK):
                    W("pe", f"t{b}")
                    do(TOKB[:, 4 * b:4 * b + 4], ps[:, b % 4 + 4, :].rearrange("p (t n) -> p t n", n=128))
                    M(f"t{b}")
                point("z")

                def own_half(dst, bank):
                    src = ps[:, bank:bank + 3, :].rearrange("p a n -> p (a n)")[:, 0:1280].rearrange("p (b q n) -> p b q n", q=2, n=128)
                    for q in range(2):
                        sl = slice(64 * q, 64 * q + 64)
                        do(dst[:, :, sl], src[:, :, q, sl])
                W("pe", "z")
                own_half(Z_, 5)
                M("z")
                point("lti")
                for lv in range(1, LEVELS):
                    point(f"la{lv}")
                    for g in rw_groups(lv):
                        n = 2 if g == 2 else 4
                        W("pe", f"X{lv}.{g}")
                        do(XM[:, 4 * g:4 * g + n], ps[:, 5 + g, 0:128 * n].rearrange("p (t n) -> p t n", n=128))
                        M(f"X{lv}.{g}")
                        W("pe", f"XT{lv}.{g}")
                        do(XTM[:, 4 * g:4 * g + n], ps[:, 2 + g, 0:128 * n].rearrange("p (t n) -> p t n", n=128))
                        M(f"XT{lv}.{g}")
                    point(f"lb{lv}")
                W("pe", "uw")
                own_half(U0, 2)
                do(WT.rearrange("p t n -> p (t n)"), ps[:, 5:7, :].rearrange("p a n -> p (a n)")[:, 0:TOK])
                M("uw")
                point("uw")
                W("pe", "sT")
                do(STS, ps[:, 2:4, :].rearrange("p a (t n) -> p (a t) n", n=128))
                M("sT")
                for c in range(PB):
                    point(f"ca{c}")
                    point(f"cb{c}")
                W("pe", "spo")
                do(SPO, ps[:, 4, 128:256])
                M("spo")
                point("su")
                W("pe", "y")
                do(yb[:, 0:512], ps[:, 6, :])
                do(yb[:, 512:640], ps[:, 7, 0:128])
                M("y")
                point("sn")
                W("pe", "sout")
                for q in range(2):
                    sl = slice(64 * q, 64 * q + 64)
                    do(SN[sl, :, sl], ps[sl, 4:6, :].rearrange("p a (t n) -> p (a t) n", n=128)[:, :, sl])
                M("sout")
                W("pe", "gate")
                do(halves(gt), two_banks(6))
                M("gate")
                point("so")
                W("ve", "var")
                do(t1, t1, ACT.Sqrt)
                M("sd")
                point("gn")
                W("ve", "y")
                if p == 4:
                    ac.wait_ge(mm_done, START[l, "z4"])
                if p == 0 and l:
                    ac.wait_ge(mm_done, START[l, "lora"])
                do(R[0][:, p % 4], yb)
                M("hi")
                point("end")

            def retention(l, h):
                W = lambda e, n: wait_mark(ac, e, l, "rt", h, n)
                M = lambda n: mark(l, "rt", h, n)
                W("pe", "tr")
                do(VT, ps[:, 0:5, :])
                for b in range(PB):
                    do(KP[:, b], ps[:, 5 + b // 2, 256 * (b % 2):256 * (b % 2) + 256], scale=H_KP[:, b:b + 1])
                do(KP[:, PB], ps[:, 7, 0:256])
                M("vk")
                W("pe", "sp")
                do(RT1[:, :, 0:512], ps[:, 5:7, :])
                M("sp")
                W("pe", f"ss{DEC_B - 1}")
                do(Y4[:, :, 0:SEQ], ps[:, 0:4, :])
                do(Y4[:, :, SEQ:TOK], ps[:, 4, :].rearrange("p (t n) -> p t n", n=128))
                M("y")
                do(VT.rearrange("p a b -> p (a b)").rearrange("p (t n) -> p t n", n=TOK), Y4, ACT.Square)
                M("ysq")
                W("ve", "var")
                do(PT[:, 0:TOK], PT[:, 0:TOK], ACT.Sqrt)
                M("sd")
                W("ve", "y")
                ac.wait_ge(mm_done, START[l, f"bb{h}"])
                do(R[0], Y4)
                M("hi")

            split(0, 0, 8)
            split(1, 1, 8)
            for l in range(DEPTH):
                ac.wait_ge(par_in, 14 * 16 * (l + 1))
                do(CR[0:NSTREAM, :], CR[0:NSTREAM, :], ACT.Silu)
                mark(l, "silu")
                wait_mark(ac, "pe", l, "par")
                do(par[:], ps[:, 0, 0:162])
                do(psh[:], ps[:, 1, 0:208])
                mark(l, "par")
                wait_mark(ac, "pe", l, "ct")
                do(CT, ps[:, 2, 0:72].rearrange("p (k s) -> p k s", s=NSTREAM))
                mark(l, "ct")
                if l == 0:
                    for b in range(NBLK):
                        wait_mark(ac, "pe", l, f"x{b}")
                        do(X[:, :, 128 * b:128 * b + 128], ps[:, 2 * (b % 4):2 * (b % 4) + 2, :].rearrange("p a (t n) -> p (a t) n", n=128))
                        mark(l, f"x{b}")
                for n in range(12):
                    m = 12 * l + n
                    ac.wait_ge(ada_used, m + 1)
                    if n >= 2:
                        ac.wait_ge(ada_turned, m - 1)
                    do(CR[0:NSTREAM, 512 * (n % 2):512 * (n % 2) + 512], ps[0:NSTREAM, 5 + n % 2, :])
                    ac.sem_inc(ada_row, 1)
                ac.wait_ge(ada_turned, 12 * (l + 1))
                do(mod[:], ps[:, 7, 0:432])
                mark(l, "mod")
                norm(l, X, S1, "0")
                high_part(l, "0", START[l, "lora"])
                ac.wait_ge(x_out, 16 * (l + 1))
                wait_mark(ac, "ve", l, "h0")
                gemm(l, "lora")
                wait_mark(ac, "ve", l, "lora")
                do(ZL[0:64, 0], ZL[0:64, 0], ACT.Tanh)
                do(ZL[:, 1], ZL[:, 1], ACT.Sigmoid)
                mark(l, "lora")
                gemm(l, "rkv0")
                for p in range(PAIRS):
                    rwkv(l, p)
                    if p % 4 == 3:
                        gemm(l, f"ba{p // 4}")
                wait_mark(ac, "ve", l, "rw", PAIRS - 1, "split")
                gemm(l, "gate0")
                ac.wait_ge(tmp_used, 48 * l + 8)
                for h in range(RH):
                    retention(l, h)
                    gemm(l, f"bb{h}")
                wait_mark(ac, "ve", l, "rt", RH - 1, "split")
                gemm(l, "gate1")
                for j in range(2):
                    ac.wait_ge(tmp_used, 48 * l + 16)
                    ac.wait_ge(mm_done, START[l, f"out{j}"])
                    do(R[0], ACC[:, 4 * j:4 * j + 4])
                    mark(l, f"mh{j}")
                    gemm(l, f"out{j}")
                wait_mark(ac, "pe", l, "nsh")
                do(NSR[0:NSTREAM, :], ps[0:NSTREAM].rearrange("p a n -> p (a n)")[:, 0:A_COLS])
                mark(l, "nsh")
                ac.wait_ge(psum_read_v, freed(START[l, "up0"], "v"))
                norm(l, S1, ACC, "m")
                wait_mark(ac, "ve", l, "x1")
                norm(l, X, S1, "1")
                high_part(l, "1", START[l, "up0"])
                wait_mark(ac, "ve", l, "h1")
                for f in range(8):
                    gemm(l, f"up{f}")
                    gemm(l, f"down{f}")
                ac.wait_ge(psum_read_v, freed(START[l, "down7"] + 8, "v"))
                norm(l, S1, ACC, "f")
            wait_mark(ac, "ve", DEPTH - 1, "x2")
            ac.wait_ge(sh_out, 32 * DEPTH)
            for b in range(NBLK):
                wait_mark(ac, "pe", DEPTH - 1, f"o{b}")
                do(XR[:, b], ps[:, 2 * (b % 4):2 * (b % 4) + 2, :].rearrange("p a n -> p (a n)"))
                mark(DEPTH - 1, f"o{b}")

        @block.vector
        def _(ve):
            mark_n, order_n = [0], [0]

            def after(ins):
                order_n[0] += 1
                ins.then_inc(ve_order, 1)
                ve.wait_ge(ve_order, order_n[0])

            tt = lambda o, a, b, op: after(ve.tensor_tensor(o, a, b, op))
            ts = lambda o, a, s1, s2, o0, o1=ALU.bypass: after(ve.tensor_scalar(o, a, s1, s2, o0, o1) if s2 is not None else ve.tensor_scalar(o, a, s1, None, o0))
            stt = lambda o, a, s, b, o0, o1: after(ve.scalar_tensor_tensor(o, a, s, b, o0, o1))
            MUL_, ADD, SUB = ALU.mult, ALU.add, ALU.subtract

            def mark(*key):
                mark_n[0] += 1
                assert VEV[key] == mark_n[0], (key, mark_n)
                ve.sem_inc(ve_mark, 1)

            def split(g, s, kt):
                ve.wait_ge(hi_done, g + 1)
                ve.tensor_tensor(WL[:, s, 0:kt], WR[:, s, 0:kt], WH[:, s, 0:kt].bitcast(F32), SUB).then_inc(lo_done, 1)

            cur_kt = [0]

            def split_next(g, s):
                if isinstance(g, int):
                    if g + 2 < TILES:
                        split(g + 2, s, KT[g + 2])
                else:
                    split(g + 2, s, cur_kt[0])

            def gemm(l, name):
                g0 = START[l, name]
                n, kt = next((j[1], j[2]) for j in jobs_of_layer() if j[0] == name)
                up0 = 32 * l + (4 * int(name[2:]) if name[:2] == "up" else 0)
                ga0 = freed(g0, "a")
                if name[:2] == "ga":
                    ve.wait_ge(psum_read_v, freed(g0, "v"))

                def tile(g, i, s):
                    par_ = i % 2 if isinstance(i, int) else (s - g0) % 2
                    src = two_banks(2 * s)
                    if name[:2] in ("ba", "bb", "ou", "do"):
                        ve.wait_ge(mm_done, g + 1)
                        dst = halves((ACC if name[0] == "b" else S1)[:, i])
                        if name[-1] == "0":
                            ve.tensor_copy(dst, src).then_inc(psum_read_v, 1)
                        else:
                            ve.wait_ge(psum_read_v, i + (freed(g0, "v") - 7))
                            ve.tensor_tensor(dst, src, dst, ADD).then_inc(psum_read_v, 1)
                    elif name == "gate0":
                        ve.wait_ge(psum_read_a, i + (ga0 + 1))
                        ve.tensor_tensor(ACC[:, i], ACC[:, i], TM[:, par_], MUL_).then_inc(tmp_used, 1)
                    elif name == "gate1":
                        ve.wait_ge(psum_read_a, i + (ga0 + 1))
                        ve.tensor_tensor(TM[:, par_], ACC[:, i], TM[:, par_], MUL_).then_inc(sq_done, 1)
                        ve.wait_ge(sq_done, i + (40 * l + 1))
                        ve.tensor_tensor(ACC[:, i], TM[:, par_], MS[:, i], ADD).then_inc(tmp_used, 1)
                    elif name[:2] == "up":
                        ve.wait_ge(psum_read_a, i + (ga0 + 1))
                        ve.tensor_tensor(FT[:, par_], TM[:, par_], TM[:, par_], MUL_).then_inc(sq_done, 1)
                        ve.wait_ge(sq_done, i + (40 * l + 8 + 4 * int(name[2:]) + 1))
                        ve.wait_ge(up_sq, i + (up0 + 1))
                        ve.tensor_tensor(R[1][:, i], FT[:, par_], R[0][:, i].bitcast(F32), SUB).then_inc(tmp_used, 1)

                def both(g, i, s):
                    tile(g, i, s)
                    split_next(g, s)
                if n != 8:
                    for i in range(n):
                        both(g0 + i, i, (g0 + i) % 2)
                    return
                cur_kt[0] = kt
                for i in range(2):
                    both(g0 + i, i, (g0 + i) % 2)
                with ve.Fori(1, n // 2 - 1) as turn:
                    for s in range(2):
                        both(turn * 2 + (g0 + s), turn * 2 + s, (g0 + s) % 2)
                for i in range(n - 2, n):
                    both(g0 + i, i, (g0 + i) % 2)

            def variance(l, tag, pe_name):
                wait_mark(ve, "pe", l, pe_name)
                ts(halves(RS), two_banks(0), 1.0 / D, EPS, MUL_, ADD)
                mark(l, "var" + tag)
                wait_mark(ve, "ac", l, "sd" + tag)
                after(ve.reciprocal(RS, RS))

            def per_stream(dst, w, op):
                a = dst[:, :, 0:SEQ]
                tt(a, a, w[:, :, 0:1].to_broadcast([128, KD, SEQ]), op)
                for b in range(DEC_B):
                    a = dst[:, :, SEQ + DEC_T * b:SEQ + DEC_T * (b + 1)]
                    tt(a, a, w[:, :, 1 + b:2 + b].to_broadcast([128, KD, DEC_T]), op)

            def pre_norm(l, tag, w, pe_name):
                variance(l, tag, pe_name)
                tt(S1, X, RS[:, None, :].to_broadcast([128, KD, TOK]), MUL_)
                per_stream(S1, MUL[:, 2 * w], MUL_)
                per_stream(S1, MOD[:, 24 * w:24 * w + 8], ADD)
                mark(l, "hx" + tag)
                wait_mark(ve, "ac", l, "hi" + tag)
                tt(H[1], S1, H[0].bitcast(F32), SUB)
                mark(l, "h" + tag)

            def post_norm(l, tag, w, pe_name, done):
                variance(l, tag, pe_name)
                tt(S1, S1, RS[:, None, :].to_broadcast([128, KD, TOK]), MUL_)
                per_stream(S1, MUL[:, 2 * w + 1], MUL_)
                tt(X, X, S1, ADD)
                mark(l, done)

            def token_shift(z, t):
                after(ve.tensor_copy(NSH[:, t, 0:1], z[:, SEQ - 1:SEQ]))
                after(ve.tensor_copy(NSH[:, t, 1:NSTREAM], z[:, SEQ + DEC_T - 1:TOK:DEC_T]))
                tt(t1[:, 1:TOK], z[:, 0:TOK - 1], z[:, 1:TOK], SUB)
                ts(t1[:, 0:1], z[:, 0:1], -1.0, None, MUL_)
                tt(t1[:, SEQ:TOK:DEC_T], PSH[:, t], z[:, SEQ:TOK:DEC_T], SUB)
                stt(z, t1, par[:, P_MU + t:P_MU + t + 1], z, MUL_, ADD)

            def rwkv(l, p):
                W = lambda e, n: wait_mark(ve, e, l, "rw", p, n)
                M = lambda n: mark(l, "rw", p, n)
                col = lambda c: par[:, c + p:c + p + 1]
                tiles_ = filler(l, p)

                def beside(i, q):
                    if q == 3:
                        g = tiles_[i][0]
                        split_next(g, g % 2)
                point = part_of(l, p, beside)
                if p:
                    ve.wait_ge(z_in, 16 * ((PAIRS - 1 + 2 * RH) * l + p))
                else:
                    ve.wait_ge(psum_read_a, freed(START[l, "rkv0"] + 3, "a"))
                for i, z in enumerate((r_b, k_b, v_b)):
                    token_shift(z, 8 * i + p)
                M("mix")
                ts(kk, k_b, col(P_KK), None, MUL_)
                tt(t1, kk, kk, MUL_)
                M("sq")
                point("sq")
                W("ac", "sig")
                ts(lam, lam, -float(np.exp(-0.5)), None, MUL_)
                after(ve.tensor_tensor_scan(cu, c1[:, C_RM:C_RM + TOK], lam, 0.0, MUL_, ADD))
                W("ac", "nr")
                ts(t1, t1, 1e-12, None, ALU.max)
                after(ve.reciprocal(t1, t1))
                tt(kk, kk, t1, MUL_)
                ts(t1, ic, -1.0, col(P_KA), ADD, MUL_)
                stt(k_b, t1, 1.0, k_b, ADD, MUL_)
                stt(t1, r_b, col(P_RK), k_b, MUL_, MUL_)
                M("rk")
                point("rk")
                W("pe", "bs")
                tt(halves(bo), two_banks(2), halves(v_b), MUL_)
                M("bo")
                after(ve.tensor_copy(MID, cu[:, 63:SEQ:128]))
                cp = cu[:, 0:SEQ].rearrange("p (c n) -> p c n", n=128)
                tt(cp, cp, MID[:, :, None].to_broadcast([128, PB, 128]), SUB)
                tt(t1, cu, lam, SUB)
                M("ea")
                tt(ic, ic, kk, MUL_)
                W("ac", "ea")
                stt(kk, kk, -1.0, t1, MUL_, MUL_)
                W("ac", "exp")
                tt(ic, ic, lam, MUL_)
                tt(k_b, k_b, lam, MUL_)
                tt(r_b, r_b, cu, MUL_)
                after(ve.tensor_copy(PC[:, 0:PB], cu[:, 127:SEQ:128]))
                after(ve.tensor_copy(PC[:, PB:PB + DEC_B], cu[:, SEQ + DEC_T - 1:TOK:DEC_T]))
                for q in range(2):
                    hm = c1[:, C_HM + q:C_HM + q + 1]
                    ts(ATR[:, :, 128 * q:128 * q + 128], kk.rearrange("p (c n) -> p c n", n=128), hm, None, MUL_)
                    ts(ATR[:, :, 256 + 128 * q:256 + 128 * q + 128], r_b.rearrange("p (c n) -> p c n", n=128), hm, None, MUL_)
                M("abkr")
                point("ab")
                for j in range(2 * NBLK):
                    b, bank = j // 2, (2, 3, 6, 7)[j % 4]
                    W("pe", f"s{j}")
                    strict, incl = (C_SUS, C_IUS) if b == PB else (C_SU, C_IU)
                    src = ps[:, bank, :].rearrange("p (t n) -> p t n", n=128)
                    for part, (dst, mk) in enumerate((((LTI, AKT)[j % 2], strict), ((BRT, KRT)[j % 2], incl))):
                        tt(dst[:, 2 * b:2 * b + 2], src[:, 2 * part:2 * part + 2],
                           c1[:, None, mk:mk + 128].to_broadcast([128, 2, 128]), MUL_)
                    M(f"s{j}")
                point("z")
                tt(LTI, LTI, ident[:, None, :].to_broadcast([128, 2 * NBLK, 128]), ADD)
                M("lti")
                point("lti")
                for g in range(3):
                    W("pe", f"lt{g}")
                    n = 2 if g == 2 else 4
                    sl = slice(4 * g, 4 * g + n)
                    bc = lambda c: c1[:, None, c:c + 128].to_broadcast([128, n, 128])
                    tt(XM[:, sl], ps[:, 2 + g, 0:128 * n].rearrange("p (t n) -> p t n", n=128), bc(C_LM), MUL_)
                    tt(XTM[:, sl], LTI[:, sl], bc(C_LMT), MUL_)
                    M(f"x0.{g}")
                for lv in range(1, LEVELS):
                    for g in rw_groups(lv):
                        W("pe", f"T{lv}.{g}")
                        n = 2 if g == 2 else 4
                        c = C_LM + 128 * lv
                        if lv == 1:
                            W("pe", "z")
                        tt(T1[:, 4 * g:4 * g + n], ps[:, 2 + g, 0:128 * n].rearrange("p (t n) -> p t n", n=128),
                           c1[:, None, c:c + 128].to_broadcast([128, n, 128]), MUL_)
                        M(f"T{lv}.{g}")
                    point(f"la{lv}")
                    point(f"lb{lv}")
                point("uw")
                for c in range(PB):
                    if c:
                        ts(SS, S, EM[:, c:c + 1], None, MUL_)
                        M(f"ss{c}")
                        W("pe", f"u{c}")
                        tt(U[:, c], ps[:, 4, 0:128], U0[:, c], ADD)
                    else:
                        W("ac", "uw")
                        after(ve.tensor_copy(U[:, 0], U0[:, 0]))
                    M(f"u{c}")
                    W("pe", f"new{c}")
                    tt(TN, ps[:, 5, 0:128], bones, MUL_)
                    if c:
                        tt(TN, TN, SS, ADD)
                    ts(S, TN, PC[:, c:c + 1], None, MUL_)
                    M(f"new{c}")
                    point(f"ca{c}")
                    point(f"cb{c}")
                e8 = c1[:, C_E8:C_E8 + 64].rearrange("p (b c) -> p b c", c=DEC_B)[:, :, :, None].to_broadcast([128, DEC_B, DEC_B, DEC_T])

                def by_stream(dst, src):
                    a = src.rearrange("p (c n) -> p c n", n=DEC_T)[:, None, :, :].to_broadcast([128, DEC_B, DEC_B, DEC_T])
                    tt(dst.rearrange("p b (c n) -> p b c n", n=DEC_T), a, e8, MUL_)
                by_stream(WM, WT[:, PB])
                M("wm")
                by_stream(RM, r_b[:, SEQ:TOK])
                for b in range(DEC_B):
                    bm = c1[:, C_BM + b:C_BM + b + 1]
                    ts(BKM[:, b], TOKB[:, 4 * PB + 1], bm, None, MUL_)
                    ts(BKM[:, 8 + b], TOKB[:, 4 * PB + 2], bm, None, MUL_)
                M("smask")
                W("pe", "su")
                tt(U[:, PB], ps[:, 5, 128:256], U0[:, PB], ADD)
                M("su")
                point("su")
                W("pe", "snew")
                tt(TNS, ps[:, 2:4, :].rearrange("p a (t n) -> p (a t) n", n=128), bones[:, None, :].to_broadcast([128, DEC_B, 128]), MUL_)
                tt(TNS, TNS, STS, ADD)
                tt(TNS, TNS, PC[:, PB:PB + DEC_B, None].to_broadcast([128, DEC_B, 128]), MUL_)
                M("snew")
                point("sn")
                W("pe", "gn1")
                stt(halves(yb), two_banks(2), -1.0 / 64, halves(yb), MUL_, ADD)
                tt(t1, yb, yb, MUL_)
                M("yc")
                point("so")
                W("pe", "gn2")
                ts(halves(t1), two_banks(4), 1.0 / 64, GN_EPS, MUL_, ADD)
                M("var")
                point("gn")
                W("ac", "sd")
                after(ve.reciprocal(t1, t1))
                tt(yb, yb, t1, MUL_)
                ts(yb, yb, col(P_LW), col(P_LB), MUL_, ADD)
                tt(yb, yb, bo, ADD)
                tt(yb, yb, gt, MUL_)
                M("y")
                W("ac", "hi")
                tt(R[1][:, p % 4], yb, R[0][:, p % 4].bitcast(F32), SUB)
                M("split")
                point("end")

            def retention(l, h):
                W = lambda e, n: wait_mark(ve, e, l, "rt", h, n)
                M = lambda n: mark(l, "rt", h, n)
                ve.wait_ge(z_in, 16 * ((PAIRS - 1 + 2 * RH) * l + PAIRS - 1 + 2 * (h + 1)))
                ve.wait_ge(ret_in, 16 * ((RH * l + h + 1) * 5 + l + 1))
                if RH * l + h and h:
                    ve.wait_ge(kp_out, 16 * (RH * l + h))
                for j in (0, 2):
                    x1, x2 = QKV[:, j], QKV[:, j + 1]
                    tt(RT1[:, 0], x2, sinT, MUL_)
                    tt(RT1[:, 1], x1, sinT, MUL_)
                    tt(x1, x1, cosT, MUL_)
                    tt(x2, x2, cosT, MUL_)
                    tt(x1, x1, RT1[:, 0], SUB)
                    tt(x2, x2, RT1[:, 1], ADD)
                tt(QD, QKV[:, 0:2, SEQ:TOK], H_QD[:, None, :].to_broadcast([128, 2, 128]), MUL_)
                M("rope")
                W("ac", "vk")
                for b in range(DEC_B):
                    ts(KS[:, b], KP[:, PB].rearrange("p (k n) -> p k n", n=128), H_KS[:, b:b + 1], None, MUL_)
                M("ks")
                at_ = 0
                for b in range(NBLK):
                    W("pe", f"s{b}")
                    n = SEQ - 128 * b if b < PB else 128
                    tt(PT[:, at_:at_ + n], ps[:, b, 0:n], H_MW[:, 0:n] if b < PB else H_MS, MUL_)
                    at_ += n
                    M(f"p{b}")
                e8 = c1[:, C_E8:C_E8 + 64].rearrange("p (b c) -> p b c", c=DEC_B)[:, :, :, None].to_broadcast([128, DEC_B, DEC_B, DEC_T])
                for k in range(2):
                    a = QD[:, k].rearrange("p (c n) -> p c n", n=DEC_T)[:, None, :, :].to_broadcast([128, DEC_B, DEC_B, DEC_T])
                    tt(QX[:, k].rearrange("p b (c n) -> p b c n", n=DEC_T), a, e8, MUL_)
                M("qx")
                g16 = float((1.0 - 2.0 ** (-5.0 - h)) ** DEC_T)
                for b in range(DEC_B):
                    n = 8 * (RH * l + h) + b
                    W("pe", f"ss{b}")
                    s = SR[:, n % 3].rearrange("p (k v) -> p k v", k=2)
                    stt(s, s, g16, ps[:, 5:7, :], MUL_, ADD)
                    M(f"ss{b}")
                W("pe", "rn")
                ts(halves(PT[:, 0:TOK]), two_banks(0), 1.0 / RV, EPS, MUL_, ADD)
                M("var")
                W("ac", "sd")
                after(ve.reciprocal(PT[:, 0:TOK], PT[:, 0:TOK]))
                tt(Y4, Y4, PT[:, None, 0:TOK].to_broadcast([128, 4, TOK]), MUL_)
                tt(Y4, Y4, SG, MUL_)
                M("y")
                W("ac", "hi")
                tt(R[1], Y4, R[0].bitcast(F32), SUB)
                M("split")

            split(0, 0, 8)
            split(1, 1, 8)
            ve.wait_ge(const_in, 16)
            for l in range(DEPTH):
                wait_mark(ve, "ac", l, "mod")
                tt(MOD, MOD, par[:, P_ADA:P_ADA + 48, None].to_broadcast([128, 48, NSTREAM]), ADD)
                for w in range(2):
                    npre = par[:, P_PRE + 8 * w:P_PRE + 8 * w + 8, None].to_broadcast([128, KD, NSTREAM])
                    npost = par[:, P_POST + 8 * w:P_POST + 8 * w + 8, None].to_broadcast([128, KD, NSTREAM])
                    stt(MUL[:, 2 * w], MOD[:, 24 * w + 8:24 * w + 16], 1.0, npre, ADD, MUL_)
                    tt(MUL[:, 2 * w + 1], MOD[:, 24 * w + 16:24 * w + 24], npost, MUL_)
                mark(l, "mod")
                pre_norm(l, "0", 0, "n0")
                gemm(l, "lora")
                ve.wait_ge(psum_read_a, freed(START[l, "rkv0"], "a"))
                token_shift(ZL[:, 0], 24)
                token_shift(ZL[:, 1], 25)
                mark(l, "lora")
                gemm(l, "rkv0")
                for p in range(PAIRS):
                    rwkv(l, p)
                    if p % 4 == 3:
                        gemm(l, f"ba{p // 4}")
                gemm(l, "gate0")
                for h in range(RH):
                    retention(l, h)
                    if h == 0:
                        ve.wait_ge(m_out, 16 * (l + 1))
                    gemm(l, f"bb{h}")
                ve.wait_ge(m_in, 32 * (l + 1))
                gemm(l, "gate1")
                for j in range(2):
                    wait_mark(ve, "ac", l, f"mh{j}")
                    ve.wait_ge(mm_done, START[l, f"out{j}"])
                    tt(R[1], ACC[:, 4 * j:4 * j + 4], R[0].bitcast(F32), SUB)
                    mark(l, f"ms{j}")
                    gemm(l, f"out{j}")
                post_norm(l, "m", 0, "mix", "x1")
                pre_norm(l, "1", 1, "n1")
                for f in range(8):
                    gemm(l, f"up{f}")
                    gemm(l, f"down{f}")
                post_norm(l, "f", 1, "ffn", "x2")


_INS = ['x_prompt', 'x_sample', 'state_shift', 'state_rwkv', 'state_ret', 'c_prompt', 'c_sample', 'ada_w', 'ada_b', 'norm_pre',
        'norm_post', 'w_in', 'a_mu', 'a_w0', 'a_w2', 'a_a0', 'a_a2', 'a_g2', 'a_kk', 'a_ka', 'a_rk', 'a_ln_w', 'a_ln_b',
        'w_branch_a', 'w_branch_b', 'w_out', 'w_ffn_up', 'w_ffn_down']
_OUTS = [(1, SEQ, D), (DEC_B, DEC_T, D), (DEPTH, 1, A_COLS), (DEPTH, 1, 16, 64, 64), (DEPTH, 1, RH, RK, RV),
         (DEPTH, DEC_B, A_COLS), (DEPTH, DEC_B, 16, 64, 64), (DEPTH, DEC_B, RH, RK, RV)]


def program(nc, shapes):
    io = {n: nc.dram_tensor(f"in_{n}_dram", s, F32, kind="ExternalInput").ap() for n, s in shapes.items()}
    outs = [nc.dram_tensor(f"out_{i}_dram", s, F32, kind="ExternalOutput").ap() for i, s in enumerate(_OUTS)]
    scratch = {n: nc.dram_tensor(f"scratch_{n}", (128, KD, TOK), F32, kind="Internal").ap() for n in ("x", "m")}
    scratch["z"] = nc.dram_tensor("scratch_z", (SPILLED, 128, TOK), F32, kind="Internal").ap()
    build(nc, io, outs, scratch)


def kernel(**inputs):
    import concourse.bacc as _bacc
    from concourse.bass_utils import run_bass_kernel_spmd as _run

    nc = _bacc.Bacc("TRN2", target_bir_lowering=False, num_devices=1)
    arrays = {n: np.ascontiguousarray(inputs[n]) for n in _INS}
    arrays["const1"], arrays["const2"] = shape_constants()
    program(nc, {n: a.shape for n, a in arrays.items()})
    r = _run(nc, [{f"in_{n}_dram": a for n, a in arrays.items()}], core_ids=[0])
    return tuple(r.results[0][f"out_{i}_dram"] for i in range(len(_OUTS)))
```

```python
import numpy as np
import concourse.bass as bass
from concourse import mybir
from contextlib import ExitStack

F32 = mybir.dt.float32
F32R = mybir.dt.float32r
ACT = mybir.ActivationFunctionType
ALU = mybir.AluOpType

D = 1024
DEPTH = 2
SEQ, DEC_B, DEC_T, PAST = 512, 8, 16, 1024
TOK = SEQ + DEC_B * DEC_T
HALF = TOK // 2
NBLK = TOK // 128
PB = SEQ // 128
KD = D // 128
A_COLS, B_COLS = 3328, 6144
A_T = A_COLS // 128
PAIRS = 8
RH, RK, RV = 4, 256, 512
FFN = 4 * D
LEVELS = 7
S_LEVELS = 4
EPS, GN_EPS = 1e-6, 64e-5
NSTREAM = 1 + DEC_B

SCR = 20508

C_ID, C_BD, C_ONE = 0, 128, 256
C_SU, C_SUS, C_IU, C_IUS = 384, 512, 640, 768
C_LM = 896
C_LMT = C_LM + 128 * LEVELS
C_HM = C_LMT + 128
C_BM = C_HM + 2
C_RM = C_BM + DEC_B
C_E8 = C_RM + TOK
NC1 = C_E8 + DEC_B * DEC_B
K_COS, K_SIN = 0, TOK
K_MW = 2 * TOK
K_MS = K_MW + RH * SEQ
K_QD = K_MS + RH * 128
K_KP = K_QD + RH * DEC_T
K_KS = K_KP + RH * PB
NC2 = K_KS + RH * DEC_B


def shape_constants():
    i = np.arange(128)
    c = np.zeros((128, NC1), np.float32)
    c[:, C_ID:C_ID + 128] = np.eye(128)
    c[:, C_BD:C_BD + 128] = (i[:, None] // 64) == (i[None, :] // 64)
    c[:, C_ONE:C_ONE + 128] = 1
    same = (i[:, None] // DEC_T) == (i[None, :] // DEC_T)
    lt, le = i[:, None] < i[None, :], i[:, None] <= i[None, :]
    c[:, C_SU:C_SU + 128], c[:, C_SUS:C_SUS + 128] = lt, lt & same
    c[:, C_IU:C_IU + 128], c[:, C_IUS:C_IUS + 128] = le, le & same
    for lv in range(LEVELS):
        m = 1 << lv
        low = (i[:, None] // (2 * m) == i[None, :] // (2 * m)) & (i[:, None] // m % 2 == 1) & (i[None, :] // m % 2 == 0)
        c[:, C_LM + 128 * lv:C_LM + 128 * lv + 128] = low | np.eye(128, dtype=bool)
        if lv == 0:
            c[:, C_LMT:C_LMT + 128] = (low | np.eye(128, dtype=bool)).T
    c[:, C_HM] = i < 64
    c[:, C_HM + 1] = i >= 64
    for b in range(DEC_B):
        c[:, C_BM + b] = i // DEC_T == b
    reset = np.ones(TOK, np.float32)
    reset[0:SEQ:128] = 0
    reset[SEQ::DEC_T] = 0
    c[:, C_RM:C_RM + TOK] = reset
    c[:, C_E8:C_E8 + DEC_B * DEC_B] = np.eye(DEC_B).reshape(-1)
    k = np.zeros((128, NC2), np.float32)
    inv = np.float32(10000.0) ** (-np.linspace(0.0, 1.0, RK // 2, dtype=np.float32))
    pos = np.concatenate([np.arange(SEQ), PAST + np.tile(np.arange(DEC_T), DEC_B)]).astype(np.float32)
    ang = (inv.astype(np.float32)[:, None] * pos[None, :]).astype(np.float32).astype(np.float64)
    k[:, K_COS:K_COS + TOK], k[:, K_SIN:K_SIN + TOK] = np.cos(ang), np.sin(ang)
    scale = float(RK) ** -0.5
    for h in range(RH):
        g = 1.0 - 2.0 ** (-5.0 - h)
        d = np.arange(SEQ)[None, :] - i[:, None]
        k[:, K_MW + SEQ * h:K_MW + SEQ * (h + 1)] = np.where(d >= 0, g ** np.maximum(d, 0), 0) * scale
        d = i[None, :] - i[:, None]
        k[:, K_MS + 128 * h:K_MS + 128 * (h + 1)] = np.where((d >= 0) & same, g ** np.maximum(d, 0), 0) * scale
        k[:, K_QD + DEC_T * h:K_QD + DEC_T * (h + 1)] = g ** (np.arange(DEC_T) + 1.0)
        for b in range(PB):
            k[:, K_KP + PB * h + b] = g ** (SEQ - 1.0 - (128 * b + i)) * scale
        for b in range(DEC_B):
            k[:, K_KS + DEC_B * h + b] = np.where(i // DEC_T == b, g ** (DEC_T - 1.0 - i % DEC_T), 0) * scale
    return c, k


Z_TILES = [6, 6, 6, 7, 5, 6, 5, 7]
Z_ALL = 12 * RH
SPILLED = Z_ALL + 3 * (PAIRS - 1) + 8

POINTS = {"sq": 3, "rk": 3, "ab": 4, "z": 2, "lti": 1, "la": 1, "lb": 1, "uw": 0, "ca": 1,
          "cb": 1, "su": 0, "sn": 1, "so": 1, "gn": 2, "end": 99}
TAIL = 6


def filler(l, p):
    out = []
    start = number_jobs()[0]
    for i in range(Z_TILES[p]):
        t = sum(Z_TILES[:p]) + i
        out.append((start[l, f"z{p}"] + i, t, t % 12 >= 8))
    if p < PAIRS - 1:
        out += [(start[l, f"rkv{p + 1}"] + i, Z_ALL + 3 * p + i, False) for i in range(3)]
    return out


def spill_number(l, p, i):
    return l * SPILLED + sum(Z_TILES[:p]) + 3 * p + i


def gate_number(l, h, i):
    return l * SPILLED + SPILLED - 8 + 2 * h + i


def jobs_of_layer():
    jobs = [("lora", 2, 8, "a"), ("rkv0", 3, 8, "a")]
    for p in range(PAIRS):
        jobs.append((f"z{p}", Z_TILES[p], 8, "a"))
        if p < PAIRS - 1:
            jobs.append((f"rkv{p + 1}", 3, 8, "a"))
        if p % 4 == 3:
            jobs.append((f"ba{p // 4}", 8, 4, "v"))
    jobs.append(("gate0", 8, 8, "a"))
    for h in range(RH):
        jobs.append((f"g{h}", 2, 8, "a"))
        jobs.append((f"bb{h}", 8, 4, "v"))
    jobs.append(("out", 8, 8, "v"))
    for f in range(8):
        jobs.append((f"up{f}", 4, 8, "a"))
        jobs.append((f"down{f}", 8, 4, "v"))
    return jobs


def number_jobs():
    start, freed_by, kt = {}, [], []
    for l in range(DEPTH):
        for name, n, k, by in jobs_of_layer():
            start[l, name] = len(freed_by)
            freed_by += [by] * n
            kt += [k] * n
    return start, freed_by, kt


def rw_groups(lv):
    return (0, 1, 2) if lv < S_LEVELS else (0, 1)


RET_PE = ["tr"] + [f"s{b}" for b in range(NBLK)] + ["sp"] + [f"ss{b}" for b in range(DEC_B)] + ["rn"]
RET_VE = ["rope", "ks"] + [f"p{b}" for b in range(NBLK)] + ["qx"] + [f"ss{b}" for b in range(DEC_B)] + ["var", "y0", "y1", "split0", "split"]
RET_AC = [f"v{b}" for b in range(NBLK)] + ["k", "sp"] + [f"ysq{v}" for v in range(4)] + ["sd", "hi0", "hi1"]


def rw_pe():
    out = ["wi", "ss", "bs"] + [f"t{b}" for b in range(NBLK)] + [f"s{j}" for j in range(2 * NBLK)] + ["z"]
    out += [f"lt{g}" for g in range(3)]
    for lv in range(1, LEVELS):
        out += [f"T{lv}.{g}" for g in rw_groups(lv)]
        out += x_marks(lv)
    out += ["uw", "sT"]
    for c in range(PB):
        out += [f"u{c}"] * (c > 0) + [f"new{c}"]
    return out + ["spo", "su", "y", "snew", "sout", "gn1", "gate", "gn2"]


def rw_ve():
    out = ["mix", "sq", "rk", "bo", "ea", "abkr"] + [f"s{j}" for j in range(2 * NBLK)] + ["lti", "x0.0", "x0.1", "x0.2"]
    for lv in range(1, LEVELS):
        out += [f"T{lv}.{g}" for g in rw_groups(lv)]
    for c in range(PB):
        out += [f"ss{c}"] * (c > 0) + [f"u{c}", f"new{c}"]
    return out + ["wm", "smask", "su", "snew", "yc", "var", "y", "split"]


def rw_ac():
    out = ["sig", "nr", "ea", "exp"] + [f"t{b}" for b in range(NBLK)] + ["z"]
    for lv in range(1, LEVELS):
        out += x_marks(lv)
    return out + ["uw", "sT", "spo", "y", "sout", "gate", "sd", "hi"]


def last_level(lv, g):
    return lv == (S_LEVELS if g == 2 else LEVELS) - 1


def x_marks(lv):
    return [f"{w}{lv}.{g}" for g in rw_groups(lv) for w in ("X", "XT")[last_level(lv, g):]]


def four(name):
    return [f"{name}.{j}" for j in range(4)]


def pre_marks(tag):
    out = []
    for j in range(5):
        out += [f"hx{tag}.{j}"] * (j < 4) + [f"h{tag}.{j - 1}"] * (j > 0)
    return out


def count_marks(head, rw, ba, ret, tail):
    out = []
    for l in range(DEPTH):
        out += [(l, n) for n in head(l)]
        for p in range(PAIRS):
            out += [(l, "rw", p, n) for n in rw]
        for h in range(RH):
            out += [(l, "rt", h, n) for n in ret]
        out += [(l, n) for n in tail(l)]
    assert len(set(out)) == len(out)
    return {k: n + 1 for n, k in enumerate(out)}


def marks_pe():
    return count_marks(lambda l: ["par", "ct"] + [f"x{b}" for b in range(NBLK)] * (l == 0) + ["shr", "n0"], rw_pe(), 0, RET_PE,
                       lambda l: ["nsh", "mix", "n1", "ffn"] + [f"o{b}" for b in range(NBLK)] * (l == DEPTH - 1))


def marks_ve():
    return count_marks(lambda l: ["mod", "var0"] + pre_marks("0") + ["lora"], rw_ve(), 0, RET_VE,
                       lambda l: ["mg0", "mg1", "ms0", "mg2", "ms1", "mg3", "ms2", "ms3", "varm"] + four("xm") + ["x1", "var1"] + pre_marks("1") + ["varf"] + four("xf") + ["x2"])


def marks_ac():
    return count_marks(lambda l: ["silu", "par", "ct"] + [f"x{b}" for b in range(NBLK)] * (l == 0) + ["mod"] + four("sq0") + ["sd0"] + four("hi0") + ["lora"],
                       rw_ac(), 0, RET_AC,
                       lambda l: ["mh0", "mh1", "mh2", "mh3", "nsh"] + four("sqm") + ["sdm"] + four("sq1") + ["sd1"] + four("hi1") + four("sqf") + ["sdf"] + [f"o{b}" for b in range(NBLK)] * (l == DEPTH - 1))


def build(nc, io, outs, scratch):
    START, FREED_BY, KT = number_jobs()
    TILES = len(FREED_BY)
    PEV, VEV, ACV = marks_pe(), marks_ve(), marks_ac()

    def freed(g, by):
        return FREED_BY[:g].count(by)

    with ExitStack() as ctx:
        def sb(name, cols, dt=F32):
            return ctx.enter_context(nc.sbuf_tensor(name, [128, cols], dt))

        def sem(name):
            return ctx.enter_context(nc.semaphore(name))

        h_hi, h_lo = sb("h_hi", KD * TOK, F32R), sb("h_lo", KD * TOK, F32R)
        r_hi, r_lo = sb("r_hi", 4 * TOK, F32R), sb("r_lo", 4 * TOK, F32R)
        w_raw, w_hi, w_lo = sb("w_raw", 2 * D), sb("w_hi", 2 * D, F32R), sb("w_lo", 2 * D, F32R)
        c1 = sb("c1", NC1)
        par = sb("par", 162)
        mod = sb("mod", 48 * NSTREAM)
        mulp = sb("mulp", 4 * 8 * NSTREAM)
        nsh = sb("nsh", A_T * NSTREAM)
        psh = sb("psh", A_T * DEC_B)
        lw = sb("lw", 2 * D)
        acc = sb("acc", KD * TOK)
        scr = sb("scr", SCR)
        ps = ctx.enter_context(nc.psum_tensor("ps", [128, 8, 512], F32))

        def tiles(buf, n=TOK):
            return buf[:].rearrange("p (t n) -> p t n", n=n)

        H = (tiles(h_hi), tiles(h_lo))
        R = (tiles(r_hi), tiles(r_lo))
        WR, WH, WL = (b[:].rearrange("p (s k n) -> p s k n", s=2, n=128) for b in (w_raw, w_hi, w_lo))
        ACC = tiles(acc)
        ident, bones, ones = c1[:, C_ID:C_ID + 128], c1[:, C_BD:C_BD + 128], c1[:, C_ONE:C_ONE + 128]
        MOD = mod[:].rearrange("p (t s) -> p t s", s=NSTREAM)
        MUL = mulp[:].rearrange("p (w t s) -> p w t s", w=4, s=NSTREAM)
        NSH = nsh[:].rearrange("p (t s) -> p t s", s=NSTREAM)
        PSH = psh[:].rearrange("p (t s) -> p t s", s=DEC_B)
        P_ADA, P_PRE, P_POST, P_MU = 0, 48, 64, 80
        P_W0, P_A0, P_KK, P_KA, P_RK, P_LW, P_LB = (106 + 8 * i for i in range(7))

        def cut(at, cols, n=None):
            v = scr[:, at:at + cols]
            return (v.rearrange("p (t n) -> p t n", n=n) if n else v), at + cols

        X, at = cut(0, KD * TOK, TOK)
        S1, at = cut(at, KD * TOK, TOK)
        AW, _ = cut(at, 2 * 4096)
        XR, at2 = cut(at, NBLK * D, D)
        TM, at3 = cut(at, 2 * TOK, TOK)
        FT, at3 = cut(at3, 2 * TOK, TOK)
        RS, at3 = cut(at3, TOK)
        at4 = 2 * KD * TOK + 8192
        PR, at4 = cut(at4, 256)
        CR, at4 = cut(at4, D)
        CT, at4 = cut(at4, 8 * NSTREAM, NSTREAM)

        ZL, at = cut(0, 2 * TOK, TOK)
        RKVZ, at = cut(at, 3 * TOK, TOK)
        r_b, k_b, v_b = RKVZ[:, 0], RKVZ[:, 1], RKVZ[:, 2]
        ic, at = cut(at, TOK)
        kk, at = cut(at, TOK)
        bo, at = cut(at, TOK)
        cu, at = cut(at, TOK)
        lam, at = cut(at, TOK)
        t1, at = cut(at, TOK)
        gt = lam
        RM, _ = cut(at - 2 * TOK, 1024, 128)
        x_at = at
        ATR, at = cut(at, NBLK * 512, 512)
        XM, _ = cut(x_at, 2 * NBLK * 128, 128)
        XTM, _ = cut(x_at + 2 * NBLK * 128, 2 * NBLK * 128, 128)
        BKM, _ = cut(x_at, 2048, 128)
        lt_at = at
        LTI, at = cut(at, 2 * NBLK * 128, 128)
        TNS, _ = cut(lt_at, 1024, 128)
        WM, _ = cut(lt_at, 1024, 128)
        ak_at = at
        AKT, at = cut(at, 2 * NBLK * 128, 128)
        STS, _ = cut(ak_at, 1024, 128)
        BRT, at = cut(at, 2 * NBLK * 128, 128)
        KRT, at = cut(at, 2 * NBLK * 128, 128)
        TOKB, at = cut(at, NBLK * 512, 128)
        S, at = cut(at, 128)
        SS, at = cut(at, 128)
        TN, at = cut(at, 128)
        PC, at = cut(at, PB + DEC_B)
        MID, at = cut(at, PB)
        EM, at = cut(at, PB)
        SN, at = cut(at, 1024, 128)
        SPO, at = cut(at, 128)
        assert at <= SCR - 2 * TOK, at
        ZT, _ = cut(SCR - 2 * TOK, 2 * TOK, TOK)
        Z_, U0, WT, U = (b.rearrange("p (t n) -> p t n", n=128) for b in (k_b, ic, kk, v_b))
        yb = cu
        T1 = AKT

        QKV, at = cut(0, 8 * TOK, TOK)
        Y4 = QKV[:, 4:8]
        YSQ, _ = cut(12 * TOK, 4 * TOK, TOK)
        VG, _ = cut(4 * TOK, 8 * TOK, TOK)
        QX = scr[:, 0:2048].rearrange("p (k b n) -> p k b n", k=2, n=128)
        SG, at = cut(at, 4 * TOK, TOK)
        VT, at = cut(at, NBLK * 512, 512)
        KP, at = cut(at, NBLK * 256, 256)
        PT, at = cut(at, 1280 + 128)
        QD, at = cut(at, 256, 128)
        SR, at = cut(at, 3 * 1024, 1024)
        SPS, at = cut(at, 2 * RV, RV)
        C2, at = cut(at, 2 * TOK + 652 + DEC_T)
        assert at <= SCR - 2 * TOK, at
        RT1, _ = cut(12 * TOK, 2 * TOK, TOK)
        KS = lw[:].rearrange("p (b k n) -> p b k n", b=DEC_B, n=128)
        HEAD_CONSTS = ((0, K_MW, SEQ), (512, K_MS, 128), (640, K_QD, DEC_T), (656, K_KP, PB), (660, K_KS, DEC_B))
        H_MW, H_MS, H_QD, H_KP, H_KS = (C2[:, 2 * TOK + a:2 * TOK + a + n] for a, _, n in HEAD_CONSTS)
        cosT, sinT = C2[:, 0:TOK], C2[:, TOK:2 * TOK]
        NSR, _ = cut(2 * KD * TOK + 3200, A_COLS)
        SHR, _ = cut(KD * TOK, A_COLS)
        MS, _ = cut(2 * KD * TOK, KD * TOK, TOK)
        G1, _ = cut(KD * TOK, KD * TOK, TOK)

        pe_mark, ve_mark, ac_mark = sem("pe_mark"), sem("ve_mark"), sem("ac_mark")
        ve_order, ac_order = sem("ve_order"), sem("ac_order")
        w_in = [sem("w_in0"), sem("w_in1")]
        hi_done, lo_done, mm_done = sem("hi_done"), sem("lo_done"), sem("mm_done")
        psum_read_a, psum_read_v = sem("psum_read_a"), sem("psum_read_v")
        tmp_used, relu_done, sq_done, up_sq = sem("tmp_used"), sem("relu_done"), sem("sq_done"), sem("up_sq")
        const_in, par_in, ada_in, x_in, ret_in, rw_in, lw_in, m_in, x_back = (
            sem("const_in"), sem("par_in"), [sem("ada_in0"), sem("ada_in1")], sem("x_in"), sem("ret_in"), sem("rw_in"),
            sem("lw_in"), sem("m_in"), sem("x_back"))
        sr_in = [sem(f"sr_in{i}") for i in range(3)]
        sr_out = [sem(f"sr_out{i}") for i in range(3)]
        shr_in = sem("shr_in")
        ada_used, ada_row, ada_turned = sem("ada_used"), sem("ada_row"), sem("ada_turned")
        z_out, z_in, qk_in, vg_in = [sem("z_out0"), sem("z_out1")], sem("z_in"), sem("qk_in"), sem("vg_in")
        x_out, m_out, rw_out, sh_out, y_out, kp_out = (
            sem("x_out"), sem("m_out"), sem("rw_out"), sem("sh_out"), sem("y_out"), sem("kp_out"))
        zero_done = sem("zero_done")

        def halves(a):
            return a.rearrange("p (h n) -> p h n", h=2)

        def two_banks(b):
            return ps[:, b:b + 2, 0:HALF]

        w_in_v = io["w_in"].rearrange("l (k p) (c n) -> l c p k n", p=128, n=128)
        up_v = io["w_ffn_up"].rearrange("l (k p) (c n) -> l c p k n", p=128, n=128)
        down_v = io["w_ffn_down"].rearrange("l (f k p) (c n) -> l f c p k n", p=128, k=4, n=128)
        ba_v = io["w_branch_a"].rearrange("l (f k p) (c n) -> l f c p k n", p=128, k=4, n=128)
        bb_v = io["w_branch_b"].rearrange("l (f k p) (c n) -> l f c p k n", p=128, k=4, n=128)
        out_v = io["w_out"].rearrange("l (k p) (c n) -> l c p k n", p=128, n=128)
        ada_v = io["ada_w"].rearrange("l (k p) (c n) -> l c p k n", p=128, n=512)

        def weight_of(l, name, i):
            if name == "lora":
                return w_in_v[l, 24 + i]
            if name.startswith("rkv"):
                return w_in_v[l, int(name[3:]) + 8 * i]
            if name == "gate0":
                return w_in_v[l, 74 + i]
            if name[0] == "g":
                return w_in_v[l, 82 + 2 * int(name[1:]) + i]
            if name == "out":
                return out_v[l, i]
            if name.startswith("z"):
                h, i = divmod(sum(Z_TILES[:int(name[1:])]) + i, 12)
                base = 26 + 2 * h + i if i < 2 else 34 + 2 * h + i - 2 if i < 4 else 42 + 4 * h + i - 4 if i < 8 else 58 + 4 * h + i - 8
                return w_in_v[l, base]
            if name.startswith("up"):
                return up_v[l, 4 * int(name[2:]) + i]
            v = {"ba": ba_v, "bb": bb_v, "do": down_v}[name[:2]]
            return v[l, int(name[-1])][i]

        def job_tiles(eng, l, name, tile, peel=0):
            g0 = START[l, name]
            n = dict((j[0], j[1]) for j in jobs_of_layer())[name]
            if n < 8 or name[0] == "z":
                for i in range(n):
                    tile(g0 + i, i, (g0 + i) % 2)
                return
            for i in range(peel):
                tile(g0 + i, i, (g0 + i) % 2)
            with eng.Fori(peel // 2, n // 2) as turn:
                for s in range(2):
                    tile(turn * 2 + (g0 + s), turn * 2 + s, (g0 + s) % 2)

        def part_of(l, p, emit):
            n, at_ = 4 * len(filler(l, p)), [0]
            tail = TAIL if p % 4 == 3 else 0

            def point(name):
                count = POINTS[name if name in POINTS else name[:2]]
                stop = n if name in ("gn", "end") else n - tail
                for _ in range(max(min(count, stop - at_[0]), 0)):
                    emit(at_[0] // 4, at_[0] % 4)
                    at_[0] += 1
            return point

        block = ctx.enter_context(nc.Block())

        def wait_mark(eng, which, *key):
            s_, v_ = {"pe": (pe_mark, PEV), "ve": (ve_mark, VEV), "ac": (ac_mark, ACV)}[which]
            eng.wait_ge(s_, v_[key])

        @block.sync
        def _(sp):
            def load_tile(l, name):
                kt = dict((j[0], j[2]) for j in jobs_of_layer())[name]

                def tile(g, i, s):
                    if isinstance(g, int) and g - 4 in spilled:
                        f, place = spilled[g - 4]
                        sp.wait_ge(psum_read_a, freed(g - 3, "a"))
                        sp.dma_start(scratch["z"][place], ZT[:, f % 2]).then_inc(z_out[f % 2], 16)
                    if not isinstance(g, int) or g >= 2:
                        sp.wait_ge(lo_done, g - 1)
                    sp.dma_start(WR[:, s, 0:kt], weight_of(l, name, i)).then_inc(w_in[s], 16)
                job_tiles(sp, l, name, tile, 4 if name[0] == "b" else 2)

            spilled = {}
            for l in range(DEPTH):
                for p in range(PAIRS):
                    for i, (g, place, _) in enumerate(filler(l, p)):
                        spilled[g] = (spill_number(l, p, i), place)
                for h in range(RH):
                    for i in range(2):
                        spilled[START[l, f"g{h}"] + i] = (gate_number(l, h, i), SPILLED - 8 + 2 * h + i)
            sp.dma_start(c1[:], io["const1"]).then_inc(const_in, 16)
            sp.dma_start(XR[:, 0:PB], io["x_prompt"][0].rearrange("(b p) n -> p b n", p=128)).then_inc(x_in, 16)
            sp.dma_start(XR[:, PB], io["x_sample"].rearrange("b t n -> (b t) n")).then_inc(x_in, 16)
            for l in range(DEPTH):
                load_tile(l, "lora")
                if l:
                    wait_mark(sp, "ve", l - 1, "x2")
                    sp.wait_ge(sh_out, 32 * l)
                else:
                    wait_mark(sp, "pe", l, "x4")
                for n in range(12):
                    m = 12 * l + n
                    if m >= 2:
                        sp.wait_ge(ada_used, m - 1)
                    sp.dma_start(AW[:, 4096 * (n % 2):4096 * (n % 2) + 4096].rearrange("p (k n) -> p k n", k=8), ada_v[l, n]
                                 ).then_inc(ada_in[n % 2], 16)
                for name, *_ in jobs_of_layer()[1:]:
                    load_tile(l, name)

        @block.gpsimd
        def _(po):
            for l in range(DEPTH):
                if l:
                    wait_mark(po, "ve", l - 1, "mg3")
                po.dma_start(CR[0:1, :], io["c_prompt"]).then_inc(par_in, 16)
                po.dma_start(CR[1:NSTREAM, :], io["c_sample"]).then_inc(par_in, 16)
                rows = [(0, "ada_b", 0), (48, "norm_pre", 0), (64, "norm_post", 0), (80, "a_mu", 0)]
                rows += [(8 * j, nm, 128) for j, nm in enumerate(["a_w0", "a_a0", "a_kk", "a_ka", "a_rk", "a_ln_w", "a_ln_b"])]
                for r0, nm, col in rows:
                    src = io[nm][l]
                    src = src.rearrange("a b -> (a b)") if len(src.shape) == 2 else src
                    n = src.shape[0] // 128
                    po.dma_start(PR[r0:r0 + n, col:col + 128], src.rearrange("(t n) -> t n", n=128)).then_inc(par_in, 16)
                po.dma_start(lw[0:64, 0:D], io["a_w2"][l]).then_inc(lw_in, 16)
                po.dma_start(lw[64:128, 0:D], io["a_a2"][l]).then_inc(lw_in, 16)
                po.dma_start(lw[:, D:2 * D], io["a_g2"][l]).then_inc(lw_in, 16)
                if l:
                    wait_mark(po, "ve", l - 1, "x2")
                    wait_mark(po, "pe", l - 1, "ffn")
                po.dma_start(SHR[0:DEC_B, :], io["state_shift"][l]).then_inc(shr_in, 16)
                if l == 0:
                    wait_mark(po, "ac", 0, "x4")
                po.dma_start(scratch["x"], X).then_inc(x_out, 16)
                wait_mark(po, "ve", l, "h0.3")
                po.wait_ge(x_out, 16 * (l + 1))
                po.memset(SN, 0.0).then_inc(zero_done, 1)
                po.wait_ge(zero_done, l + 1)
                for p in range(PAIRS):
                    n = 8 * l + p
                    if p:
                        for i in range(3):
                            f = spill_number(l, p - 1, Z_TILES[p - 1] + i)
                            po.wait_ge(z_out[f % 2], 16 * (f // 2 + 1))
                        po.dma_start(RKVZ, scratch["z"][Z_ALL + 3 * (p - 1):Z_ALL + 3 * p].rearrange("t p n -> p t n")
                                     ).then_inc(z_in, 16)
                        po.wait_ge(rw_out, 64 * n)
                    for q in range(2):
                        sl = slice(64 * q, 64 * q + 64)
                        po.dma_start(SN[sl, :, sl], io["state_rwkv"][l, :, 2 * p + q].rearrange("b v k -> v b k")).then_inc(rw_in, 16)
                    wait_mark(po, "ac", l, "rw", p, "sout")
                    for q in range(2):
                        sl = slice(64 * q, 64 * q + 64)
                        po.dma_start(outs[6][l, :, 2 * p + q].rearrange("b v k -> v b k"), SN[sl, :, sl]).then_inc(rw_out, 16)
                        po.dma_start(outs[3][l, 0, 2 * p + q], SPO[sl, sl]).then_inc(rw_out, 16)
                wait_mark(po, "ve", l, "rw", PAIRS - 1, "split")
                po.wait_ge(rw_out, 64 * 8 * (l + 1))
                po.dma_start(C2[:, 0:2 * TOK], io["const2"][:, 0:2 * TOK]).then_inc(ret_in, 16)

                def queries_and_keys(h):
                    for i in range(2):
                        f = spill_number(l, PAIRS - 1, Z_TILES[-1] - 2 + i)
                        po.wait_ge(z_out[f % 2], 16 * (f // 2 + 1))
                    po.dma_start(QKV[:, 0:4], scratch["z"][12 * h:12 * h + 4].rearrange("t p n -> p t n")).then_inc(qk_in, 16)
                    for a, src, n in HEAD_CONSTS:
                        po.dma_start(C2[:, 2 * TOK + a:2 * TOK + a + n], io["const2"][:, src + n * h:src + n * (h + 1)]).then_inc(ret_in, 16)

                queries_and_keys(0)
                for h in range(RH):
                    if h:
                        wait_mark(po, "ve", l, "rt", h - 1, "split")
                    po.dma_start(VG, scratch["z"][12 * h + 4:12 * h + 12].rearrange("t p n -> p t n")).then_inc(vg_in, 16)
                    if h == 0:
                        po.wait_ge(tmp_used, 40 * l + 8)
                        po.dma_start(scratch["m"], ACC).then_inc(m_out, 16)
                    for b in range(DEC_B):
                        n = 8 * (RH * l + h) + b
                        if n >= 3:
                            po.wait_ge(sr_out[n % 3], 16 * (n // 3))
                        po.dma_start(SR[:, n % 3].rearrange("p (k v) -> p k v", k=2),
                                     io["state_ret"][l, b, h].rearrange("(k p) v -> p k v", p=128)).then_inc(sr_in[n % 3], 16)
                    wait_mark(po, "ac", l, "rt", h, "sp")
                    po.dma_start(outs[4][l, 0, h].rearrange("(k p) v -> p k v", p=128), SPS).then_inc(kp_out, 16)
                    if h < RH - 1:
                        wait_mark(po, "ve", l, "rt", h, f"ss{DEC_B - 1}")
                        queries_and_keys(h + 1)
                wait_mark(po, "ve", l, "rt", RH - 1, "split")
                po.wait_ge(kp_out, 16 * RH * (l + 1))
                for i in range(3):
                    po.wait_ge(sr_out[i], 16 * ((32 * (l + 1) - i + 2) // 3))
                po.wait_ge(m_out, 16 * (l + 1))
                for i in range(2):
                    f = gate_number(l, RH - 1, i)
                    po.wait_ge(z_out[f % 2], 16 * (f // 2 + 1))
                for t in range(KD):
                    po.wait_ge(psum_read_v, freed(START[l, f"bb{RH - 1}"] + t, "v"))
                    po.dma_start(MS[:, t], scratch["m"][:, t]).then_inc(m_in, 16)
                    po.dma_start(G1[:, t], scratch["z"][SPILLED - 8 + t]).then_inc(m_in, 16)
                wait_mark(po, "ve", l, "mg3")
                po.dma_start(X, scratch["x"]).then_inc(x_back, 16)
                wait_mark(po, "ac", l, "nsh")
                po.dma_start(outs[2][l], NSR[0:1, :]).then_inc(sh_out, 16)
                po.dma_start(outs[5][l], NSR[1:NSTREAM, :]).then_inc(sh_out, 16)
            for b in range(NBLK):
                wait_mark(po, "ac", DEPTH - 1, f"o{b}")
                dst = outs[0][0, 128 * b:128 * b + 128] if b < PB else outs[1].rearrange("b t n -> (b t) n")
                po.dma_start(dst, XR[:, b]).then_inc(y_out, 16)
            po.wait_ge(y_out, 16 * NBLK)
            po.wait_ge(sh_out, 32 * DEPTH)

        @block.tensor
        def _(pe):
            mark_n = [0]

            def mark(ins, *key):
                mark_n[0] += 1
                assert PEV[key] == mark_n[0], (key, mark_n)
                ins.then_inc(pe_mark, 1)

            def mm(out, lhsT, rhs, start=True, stop=True):
                return pe.matmul(out, lhsT, rhs, start=start, stop=stop, skip_group_check=True)

            def tr(out, in_):
                n = in_.shape[0]
                return pe.transpose(out, in_, c1[0:n, C_ID:C_ID + n])

            def psum_clear(g):
                pe.wait_ge(psum_read_a, freed(g, "a"))
                if freed(g, "v"):
                    pe.wait_ge(psum_read_v, freed(g, "v"))

            def gemm(l, name, parts=()):
                g0 = START[l, name]
                kt = dict((j[0], j[2]) for j in jobs_of_layer())[name]
                by = FREED_BY[g0]
                hi, lo = R if kt == 4 else H
                behind = name in ("rkv0", "gate0", "out") or name[:2] in ("bb", "do") or (name[:2] == "up" and name != "up0")
                if not behind or parts:
                    psum_clear(g0)

                def step(s, k):
                    for n_, (w, x) in enumerate(((WH, hi), (WH, lo), (WL, hi))):
                        for hf in range(2):
                            last = mm(ps[:, 2 * s + hf, 0:HALF], w[:, s, k], x[:, k, HALF * hf:HALF * hf + HALF],
                                      start=(k == 0 and n_ == 0), stop=(k == kt - 1 and n_ == 2))
                    return last

                if parts:
                    pe.wait_ge(lo_done, g0 + 2)
                    for j, part in enumerate(parts):
                        wait_mark(pe, "ve", *part)
                        for t in range(2):
                            for k in (2 * j, 2 * j + 1):
                                last = step((g0 + t) % 2, k)
                            if j == len(parts) - 1:
                                last.then_inc(mm_done, 1)

                def tile(g, i, s):
                    if parts and isinstance(i, int) and i < 2:
                        return
                    pe.wait_ge(lo_done, g + 1)
                    if not isinstance(i, int) or i >= 2:
                        pe.wait_ge(psum_read_a if by == "a" else psum_read_v, i + (freed(g0, by) - 1))
                    elif behind:
                        psum_clear(g - 1)
                    for k in range(kt):
                        if name[:2] == "do" and isinstance(i, int) and i == 0:
                            pe.wait_ge(tmp_used, 40 * l + 8 + 4 * int(name[-1]) + k + 1)
                        last = step(s, k)
                    last.then_inc(mm_done, 1)
                job_tiles(pe, l, name, tile, 2)

            def channel_sums(mat, src, n, bank):
                for hf in range(2):
                    for i in range(n):
                        last = mm(ps[:, bank + hf, 0:HALF], mat, src[:, i, HALF * hf:HALF * hf + HALF], i == 0, i == n - 1)
                return last

            def rwkv(l, p):
                W = lambda e, n: wait_mark(pe, e, l, "rw", p, n)
                M = lambda ins, n: mark(ins, l, "rw", p, n)
                tiles_ = filler(l, p)

                def quarter(i, q):
                    g = tiles_[i][0]
                    if q == 0:
                        pe.wait_ge(lo_done, g + 1)
                        psum_clear(g)
                    for k in (2 * q, 2 * q + 1):
                        for n_, (w, x) in enumerate(((WH, H[0]), (WH, H[1]), (WL, H[0]))):
                            for hf in range(2):
                                last = mm(ps[:, hf, 0:HALF], w[:, g % 2, k], x[:, k, HALF * hf:HALF * hf + HALF],
                                          start=(k == 0 and n_ == 0), stop=(k == 7 and n_ == 2))
                    if q == 3:
                        last.then_inc(mm_done, 1)
                point = part_of(l, p, quarter)
                if p % 4 == 0:
                    psum_clear(START[l, f"z{p}"])
                else:
                    wait_mark(pe, "ve", l, "rw", p - 1, "var")
                ch = slice(128 * p, 128 * p + 128)
                for hf in range(2):
                    mm(ps[:, 2 + hf, 0:HALF], lw[0:64, ch], ZL[0:64, 0, HALF * hf:HALF * hf + HALF])
                for hf in range(2):
                    last = mm(ps[:, 4 + hf, 0:HALF], lw[64:128, ch], ZL[64:128, 0, HALF * hf:HALF * hf + HALF])
                M(last, "wi")
                point("sq")
                W("ve", "sq")
                if p % 4:
                    wait_mark(pe, "ac", l, "rw", p - 1, "gate")
                M(channel_sums(bones, t1[:, None, :], 1, 6), "ss")
                point("rk")
                W("ve", "rk")
                W("ac", "sig")
                M(channel_sums(bones, t1[:, None, :], 1, 2), "bs")
                point("ab")
                W("ve", "abkr")
                W("ac", "nr")
                for b in range(NBLK):
                    if b == 4:
                        W("ac", "t0")
                    for j, src in enumerate((kk, ic, k_b, v_b)):
                        last = tr(ps[:, b % 4 + 4, 128 * j:128 * j + 128], src[:, 128 * b:128 * b + 128])
                    M(last, f"t{b}")
                for j in range(2 * NBLK):
                    b, w = j // 2, (ic, k_b)[j % 2]
                    if j >= 4:
                        W("ve", f"s{j - 4}")
                    elif j >= 2:
                        W("ac", f"t{j}")
                    M(mm(ps[:, (2, 3, 6, 7)[j % 4], :], w[:, 128 * b:128 * b + 128], ATR[:, b]), f"s{j}")
                W("ac", f"t{NBLK - 1}")
                point("z")
                W("ve", f"s{2 * NBLK - 1}")

                def flat(bank, c, n):
                    return ps[:, bank + c // 512, c % 512:c % 512 + n]
                for m in range(2 * NBLK):
                    last = mm(flat(5, 128 * m, 128), AKT[:, m], TOKB[:, 4 * (m // 2) + 3])
                M(last, "z")
                point("lti")
                W("ve", "lti")
                for g in range(3):
                    for m in range(4 * g, min(4 * g + 4, 2 * NBLK)):
                        last = tr(ps[:, 2 + g, 128 * (m % 4):128 * (m % 4) + 128], LTI[:, m])
                    M(last, f"lt{g}")
                W("ac", "z")
                tb, xb_ = (2, 3, 4), (5, 6, 7)
                for lv in range(1, LEVELS):
                    for g in rw_groups(lv):
                        if lv == 1:
                            W("ve", f"x0.{g}")
                        else:
                            W("ac", f"XT{lv - 1}.{g}")
                        for m in range(4 * g, min(4 * g + 4, 2 * NBLK)):
                            last = mm(ps[:, tb[g], 128 * (m % 4):128 * (m % 4) + 128], LTI[:, m], XM[:, m])
                        M(last, f"T{lv}.{g}")
                    point(f"la{lv}")
                    for g in rw_groups(lv):
                        W("ve", f"T{lv}.{g}")
                        if not last_level(lv, g):
                            for m in range(4 * g, min(4 * g + 4, 2 * NBLK)):
                                last = mm(ps[:, xb_[g], 128 * (m % 4):128 * (m % 4) + 128], XTM[:, m], T1[:, m])
                            M(last, f"X{lv}.{g}")
                        for m in range(4 * g, min(4 * g + 4, 2 * NBLK)):
                            last = mm(ps[:, tb[g], 128 * (m % 4):128 * (m % 4) + 128], T1[:, m], XTM[:, m])
                        M(last, f"XT{lv}.{g}")
                    point(f"lb{lv}")
                W("ac", f"XT{S_LEVELS - 1}.2")
                for g in (0, 1):
                    W("ac", f"XT{LEVELS - 1}.{g}")
                for m in range(2 * NBLK):
                    b, q = m // 2, m % 2
                    mm(flat(2, 128 * m, 128), XTM[:, m], Z_[:, b])
                    last = mm(flat(5, 128 * b, 128)[64 * q:64 * q + 64], TOKB[:, 4 * b, 64 * q:64 * q + 64], XTM[:, m])
                M(last, "uw")
                point("uw")
                pe.wait_ge(rw_in, 32 * (8 * l + p + 1))
                W("ac", "uw")
                for b in range(DEC_B):
                    last = tr(flat(2, 128 * b, 128), SN[:, b])
                M(last, "sT")

                def own_terms(bank, c0, b, first):
                    for q in range(2):
                        sl, o = slice(64 * q, 64 * q + 64), ps[64 * q:64 * q + 64, bank, c0:c0 + 128]
                        mm(o, U[:, b, sl], BRT[:, 2 * b + q], first, False)
                        last = mm(o, TOKB[:, 4 * b + 3, sl], KRT[:, 2 * b + q], False, True)
                    return last

                for c in range(PB):
                    t = slice(128 * c, 128 * c + 128)
                    if c:
                        W("ve", f"ss{c}")
                        M(mm(ps[:, 4, 0:128], WT[:, c], SS), f"u{c}")
                        mm(ps[:, 6, t], SS, r_b[:, t], True, False)
                    point(f"ca{c}")
                    W("ve", f"u{c}")
                    mm(ps[:, 5, 0:128], TOKB[:, 4 * c + 1], U[:, c], True, False)
                    M(mm(ps[:, 5, 0:128], TOKB[:, 4 * c + 2], TOKB[:, 4 * c + 3], False, True), f"new{c}")
                    own_terms(6, 128 * c, c, c == 0)
                    point(f"cb{c}")
                W("ve", f"new{PB - 1}")
                M(tr(ps[:, 4, 128:256], S), "spo")
                W("ac", "sT")
                W("ve", "smask")
                for b in range(DEC_B):
                    last = mm(ps[:, 5, 128:256], WM[:, b], STS[:, b], b == 0, b == DEC_B - 1)
                M(last, "su")
                for b in range(DEC_B):
                    mm(ps[:, 7, 0:128], STS[:, b], RM[:, b], b == 0, False)
                point("su")
                W("ve", "su")
                M(own_terms(7, 0, PB, False), "y")
                for b in range(DEC_B):
                    mm(flat(2, 128 * b, 128), BKM[:, b], U[:, PB], True, False)
                    last = mm(flat(2, 128 * b, 128), BKM[:, 8 + b], TOKB[:, 4 * PB + 3], False, True)
                M(last, "snew")
                point("sn")
                W("ve", "snew")
                W("ac", "spo")
                for b in range(DEC_B):
                    last = tr(flat(4, 128 * b, 128), TNS[:, b])
                M(last, "sout")
                W("ac", "y")
                M(channel_sums(bones, yb[:, None, :], 1, 2), "gn1")
                for hf in range(2):
                    last = mm(ps[:, 6 + hf, 0:HALF], lw[:, D + 128 * p:D + 128 * p + 128], ZL[:, 1, HALF * hf:HALF * hf + HALF])
                M(last, "gate")
                point("so")
                W("ve", "yc")
                W("ac", "sout")
                M(channel_sums(bones, t1[:, None, :], 1, 4), "gn2")
                point("gn")
                point("end")

            def retention(l, h):
                W = lambda e, n: wait_mark(pe, e, l, "rt", h, n)
                M = lambda ins, n: mark(ins, l, "rt", h, n)
                psum_clear(START[l, f"g{h}"])
                W("ve", "rope")
                pe.wait_ge(vg_in, 16 * (RH * l + h + 1))
                for b in range(NBLK):
                    t = slice(128 * b, 128 * b + 128)
                    for j in range(4):
                        tr(ps[:, b, 128 * j:128 * j + 128], QKV[:, 4 + j, t])
                    for j in range(2):
                        last = tr(ps[:, 5 + b // 2, 256 * (b % 2) + 128 * j:256 * (b % 2) + 128 * j + 128], QKV[:, 2 + j, t])
                M(last, "tr")
                for b in range(NBLK):
                    W("ac", f"v{b}")
                    n = SEQ - 128 * b if b < PB else 128
                    for j in range(2):
                        last = mm(ps[:, b, 0:n], QKV[:, 2 + j, 128 * b:128 * b + 128], QKV[:, j, 128 * b:128 * b + n], j == 0, j == 1)
                    M(last, f"s{b}")
                W("ac", "k")
                for k in range(2):
                    for b in range(PB):
                        last = mm(ps[:, 5 + k, :], KP[:, b, 128 * k:128 * k + 128], VT[:, b], b == 0, b == PB - 1)
                M(last, "sp")
                for b in range(NBLK):
                    W("ve", f"p{b}")
                for v in range(4):
                    at_ = 0
                    for b in range(PB):
                        n = SEQ - 128 * b
                        mm(ps[:, v, 128 * b:512], VT[:, b, 128 * v:128 * v + 128], PT[:, at_:at_ + n], b == 0, b == PB - 1)
                        at_ += n
                for v in range(4):
                    mm(ps[:, 4, 128 * v:128 * v + 128], VT[:, PB, 128 * v:128 * v + 128], PT[:, 1280:1408], v == 0, False)
                W("ve", "ks")
                W("ve", "qx")
                W("ac", "sp")
                for b in range(DEC_B):
                    n = 8 * (RH * l + h) + b
                    pe.wait_ge(sr_in[n % 3], 16 * (n // 3 + 1))
                    for v in range(4):
                        for k in range(2):
                            c = 512 * k + 128 * v
                            mm(ps[:, 4, 128 * v:128 * v + 128], SR[:, n % 3, c:c + 128], QX[:, k, b], False, b == DEC_B - 1 and k == 1)
                    if b:
                        W("ve", f"ss{b - 1}")
                    for k in range(2):
                        last = mm(ps[:, 5 + k, :], KS[:, b, k], VT[:, PB])
                    M(last, f"ss{b}")
                W("ve", f"ss{DEC_B - 1}")
                for v in range(4):
                    W("ac", f"ysq{v}")
                    for hf in range(2):
                        last = mm(ps[:, 5 + hf, 0:HALF], ones, YSQ[:, v, HALF * hf:HALF * hf + HALF], v == 0, v == 3)
                M(last, "rn")

            def norm_sums(l, name, wait, src):
                for j in range(4):
                    wait_mark(pe, "ac", l, f"{wait}.{j}")
                    for i in (2 * j, 2 * j + 1):
                        for hf in range(2):
                            last = mm(ps[:, hf, 0:HALF], ones, src[:, i, HALF * hf:HALF * hf + HALF], i == 0, i == KD - 1)
                mark(last, l, name)

            pe.wait_ge(const_in, 16)
            for l in range(DEPTH):
                pe.wait_ge(par_in, 13 * 16 * (l + 1))
                if l:
                    wait_mark(pe, "ve", l - 1, "varf")
                tr(ps[:, 0, 0:106], PR[0:106, 0:128])
                last = tr(ps[:, 0, 106:162], PR[0:56, 128:256])
                mark(last, l, "par")
                wait_mark(pe, "ac", l, "silu")
                for k in range(KD):
                    last = tr(ps[:, 2, NSTREAM * k:NSTREAM * k + NSTREAM], CR[0:NSTREAM, 128 * k:128 * k + 128])
                mark(last, l, "ct")
                if l == 0:
                    pe.wait_ge(x_in, 32)
                    wait_mark(pe, "ac", l, "par")
                    wait_mark(pe, "ac", l, "ct")
                    for b in range(NBLK):
                        if b == 4:
                            wait_mark(pe, "ac", l, "x0")
                        for k in range(KD):
                            last = tr(ps[:, 2 * (b % 4) + k // 4, 128 * (k % 4):128 * (k % 4) + 128], XR[:, b, 128 * k:128 * k + 128])
                        mark(last, l, f"x{b}")
                    wait_mark(pe, "ac", l, "x4")
                wait_mark(pe, "ac", l, "par")
                wait_mark(pe, "ac", l, "ct")
                for n in range(13):
                    m = 12 * l + n
                    if n < 12:
                        pe.wait_ge(ada_in[n % 2], 16 * (6 * l + n // 2 + 1))
                        if n >= 2:
                            pe.wait_ge(ada_row, m - 1)
                        a = AW[:, 4096 * (n % 2):4096 * (n % 2) + 4096].rearrange("p (k n) -> p k n", k=8)
                        for k in range(KD):
                            last = mm(ps[0:NSTREAM, 5 + n % 2, :], CT[:, k], a[:, k], k == 0, k == KD - 1)
                        last.then_inc(ada_used, 1)
                    if n:
                        pe.wait_ge(ada_row, m)
                        for j in range(4):
                            t = 4 * (n - 1) + j
                            last = tr(ps[:, 7, NSTREAM * t:NSTREAM * t + NSTREAM], CR[0:NSTREAM, 512 * ((n - 1) % 2) + 128 * j:512 * ((n - 1) % 2) + 128 * j + 128])
                        last.then_inc(ada_turned, 1)
                pe.wait_ge(shr_in, 16 * (l + 1))
                for t in range(A_T):
                    last = tr(ps[:, 2, 8 * t:8 * t + 8], SHR[0:DEC_B, 128 * t:128 * t + 128])
                mark(last, l, "shr")
                wait_mark(pe, "ac", l, "mod")
                norm_sums(l, "n0", "sq0", S1)
                gemm(l, "lora", [(l, f"h0.{j}") for j in range(4)])
                gemm(l, "rkv0")
                wait_mark(pe, "ac", l, "lora")
                pe.wait_ge(lw_in, 48 * (l + 1))
                for p in range(PAIRS):
                    rwkv(l, p)
                    if p % 4 == 3:
                        wait_mark(pe, "ve", l, "rw", p, "split")
                        gemm(l, f"ba{p // 4}")
                gemm(l, "gate0")
                for h in range(RH):
                    retention(l, h)
                    gemm(l, f"g{h}")
                    gemm(l, f"bb{h}", [(l, "rt", h, "split0"), (l, "rt", h, "split")])
                gemm(l, "out", [(l, f"ms{j}") for j in range(4)])
                psum_clear(START[l, "up0"])
                for t in range(A_T):
                    last = tr(ps[0:NSTREAM, t // 4, 128 * (t % 4):128 * (t % 4) + 128], NSH[:, t])
                mark(last, l, "nsh")
                wait_mark(pe, "ac", l, "nsh")
                norm_sums(l, "mix", "sqm", ACC)
                wait_mark(pe, "ve", l, "varm")
                norm_sums(l, "n1", "sq1", S1)
                for f in range(8):
                    gemm(l, f"up{f}", [(l, f"h1.{j}") for j in range(4)] if f == 0 else ())
                    gemm(l, f"down{f}")
                psum_clear(START[l, "down7"] + 8)
                norm_sums(l, "ffn", "sqf", ACC)
            wait_mark(pe, "ve", DEPTH - 1, "x2")
            for b in range(NBLK):
                if b == 4:
                    wait_mark(pe, "ac", DEPTH - 1, "o0")
                for k in range(KD):
                    last = tr(ps[:, 2 * (b % 4) + k // 4, 128 * (k % 4):128 * (k % 4) + 128], X[:, k, 128 * b:128 * b + 128])
                mark(last, DEPTH - 1, f"o{b}")

        @block.scalar
        def _(ac):
            mark_n, order_n = [0], [0]

            def do(out, in_, f=ACT.Copy, **kw):
                order_n[0] += 1
                ac.activation(out, in_, f, **kw).then_inc(ac_order, 1)
                ac.wait_ge(ac_order, order_n[0])

            def mark(*key):
                mark_n[0] += 1
                assert ACV[key] == mark_n[0], (key, mark_n)
                ac.sem_inc(ac_mark, 1)

            def split(g, s, kt):
                ac.wait_ge(w_in[s], (g - s) * 8 + 16)
                if not isinstance(g, int) or g >= 2:
                    ac.wait_ge(mm_done, g - 1)
                ac.activation(WH[:, s, 0:kt], WR[:, s, 0:kt], ACT.Copy).then_inc(hi_done, 1)

            def gemm(l, name):
                g0, n, kt = START[l, name], *next((j[1], j[2]) for j in jobs_of_layer() if j[0] == name)
                t0 = 40 * l + (8 + 4 * int(name[2:]) if name[:2] == "up" else 0)

                def tile(g, i, s):
                    par_ = i % 2 if isinstance(i, int) else (s - g0) % 2
                    if FREED_BY[g0] == "a":
                        ac.wait_ge(mm_done, g + 1)
                        src = two_banks(2 * s)
                        if name == "lora":
                            ac.activation(halves(ZL[:, i]), src, ACT.Copy).then_inc(psum_read_a, 1)
                        elif name.startswith("rkv"):
                            ac.activation(halves(RKVZ[:, i]), src, ACT.Copy).then_inc(psum_read_a, 1)
                        elif name == "gate0":
                            if not isinstance(i, int) or i >= 2:
                                ac.wait_ge(tmp_used, i + (t0 - 1))
                            ac.activation(halves(ZT[:, par_]), src, ACT.Sigmoid).then_inc(psum_read_a, 1)
                        else:
                            ac.wait_ge(tmp_used, i + (t0 - 1))
                            ac.activation(halves(TM[:, par_]), src, ACT.Relu).then_inc(psum_read_a, 1)
                            ac.wait_ge(psum_read_a, freed(g, "a") + 1)
                            ac.activation(R[0][:, i], TM[:, par_], ACT.Square).then_inc(up_sq, 1)
                job_tail(l, name, tile)

            def job_tail(l, name, tile):
                g0 = START[l, name]

                def both(g, i, s):
                    tile(g, i, s)
                    split_next(g, s)
                job_tiles_ve(ac, l, name, both)

            def split_next(g, s):
                if isinstance(g, int):
                    if g + 2 < TILES:
                        split(g + 2, s, KT[g + 2])
                else:
                    split(g + 2, s, cur_kt[0])

            cur_kt = [0]

            def job_tiles_ve(eng, l, name, tile):
                g0 = START[l, name]
                n, kt = next((j[1], j[2]) for j in jobs_of_layer() if j[0] == name)
                if n != 8:
                    for i in range(n):
                        tile(g0 + i, i, (g0 + i) % 2)
                    return
                cur_kt[0] = kt
                for i in range(2):
                    tile(g0 + i, i, (g0 + i) % 2)
                with eng.Fori(1, n // 2 - 1) as turn:
                    for s in range(2):
                        tile(turn * 2 + (g0 + s), turn * 2 + s, (g0 + s) % 2)
                for i in range(n - 2, n):
                    tile(g0 + i, i, (g0 + i) % 2)

            def norm(l, src, sq, tag, ready=None):
                for j in range(4):
                    two = slice(2 * j, 2 * j + 2)
                    if ready:
                        ready(j)
                    do(sq[:, two], src[:, two], ACT.Square)
                    mark(l, f"sq{tag}.{j}")
                wait_mark(ac, "ve", l, "var" + tag)
                do(RS, RS, ACT.Sqrt)
                mark(l, "sd" + tag)

            def high_part(l, tag, g):
                if g:
                    ac.wait_ge(mm_done, g)
                w = int(tag)
                for j in range(4):
                    wait_mark(ac, "ve", l, f"hx{tag}.{j}")
                    for t in (2 * j, 2 * j + 1):
                        do(S1[:, t, 0:SEQ], S1[:, t, 0:SEQ], ACT.Identity, scale=MUL[:, 2 * w, t, 0:1], bias=MOD[:, 24 * w + t, 0:1])
                    do(H[0][:, 2 * j:2 * j + 2], S1[:, 2 * j:2 * j + 2])
                    mark(l, f"hi{tag}.{j}")

            def rwkv(l, p):
                W = lambda e, n: wait_mark(ac, e, l, "rw", p, n)
                M = lambda n: mark(l, "rw", p, n)
                col = lambda c: par[:, c + p:c + p + 1]
                tiles_ = filler(l, p)

                def beside(i, q):
                    if q == 3:
                        g, _, gate = tiles_[i]
                        f = spill_number(l, p, i)
                        if f >= 2:
                            ac.wait_ge(z_out[f % 2], 16 * (f // 2))
                        ac.wait_ge(mm_done, g + 1)
                        ac.activation(halves(ZT[:, f % 2]), two_banks(0), ACT.Silu if gate else ACT.Copy).then_inc(psum_read_a, 1)
                        split_next(g, g % 2)
                point = part_of(l, p, beside)
                W("pe", "wi")
                do(halves(lam), two_banks(2), ACT.Sigmoid, bias=col(P_W0))
                do(halves(ic), two_banks(4), ACT.Sigmoid, bias=col(P_A0))
                M("sig")
                point("sq")
                W("pe", "ss")
                do(halves(t1), two_banks(6), ACT.Sqrt)
                M("nr")
                point("rk")
                W("ve", "ea")
                do(t1, t1, ACT.Exp)
                M("ea")
                do(lam, cu, ACT.Exp, scale=-1.0)
                do(EM, MID, ACT.Exp)
                do(cu, cu, ACT.Exp)
                M("exp")
                point("ab")
                for b in range(NBLK):
                    W("pe", f"t{b}")
                    do(TOKB[:, 4 * b:4 * b + 4], ps[:, b % 4 + 4, :].rearrange("p (t n) -> p t n", n=128))
                    M(f"t{b}")
                point("z")

                def own_half(dst, bank):
                    src = ps[:, bank:bank + 3, :].rearrange("p a n -> p (a n)")[:, 0:1280].rearrange("p (b q n) -> p b q n", q=2, n=128)
                    for q in range(2):
                        sl = slice(64 * q, 64 * q + 64)
                        do(dst[:, :, sl], src[:, :, q, sl])
                W("pe", "z")
                own_half(Z_, 5)
                M("z")
                point("lti")
                for lv in range(1, LEVELS):
                    point(f"la{lv}")
                    for g in rw_groups(lv):
                        n = 2 if g == 2 else 4
                        if not last_level(lv, g):
                            W("pe", f"X{lv}.{g}")
                            do(XM[:, 4 * g:4 * g + n], ps[:, 5 + g, 0:128 * n].rearrange("p (t n) -> p t n", n=128))
                            M(f"X{lv}.{g}")
                        W("pe", f"XT{lv}.{g}")
                        do(XTM[:, 4 * g:4 * g + n], ps[:, 2 + g, 0:128 * n].rearrange("p (t n) -> p t n", n=128))
                        M(f"XT{lv}.{g}")
                    point(f"lb{lv}")
                W("pe", "uw")
                own_half(U0, 2)
                do(WT.rearrange("p t n -> p (t n)"), ps[:, 5:7, :].rearrange("p a n -> p (a n)")[:, 0:TOK])
                M("uw")
                point("uw")
                W("pe", "sT")
                do(STS, ps[:, 2:4, :].rearrange("p a (t n) -> p (a t) n", n=128))
                M("sT")
                for c in range(PB):
                    point(f"ca{c}")
                    point(f"cb{c}")
                W("pe", "spo")
                do(SPO, ps[:, 4, 128:256])
                M("spo")
                point("su")
                W("pe", "y")
                do(yb[:, 0:512], ps[:, 6, :])
                do(yb[:, 512:640], ps[:, 7, 0:128])
                M("y")
                point("sn")
                W("pe", "sout")
                for q in range(2):
                    sl = slice(64 * q, 64 * q + 64)
                    do(SN[sl, :, sl], ps[sl, 4:6, :].rearrange("p a (t n) -> p (a t) n", n=128)[:, :, sl])
                M("sout")
                W("pe", "gate")
                do(halves(gt), two_banks(6))
                M("gate")
                point("so")
                W("ve", "var")
                do(t1, t1, ACT.Sqrt)
                M("sd")
                point("gn")
                W("ve", "y")
                if p == 4:
                    ac.wait_ge(mm_done, START[l, "z4"])
                if p == 0 and l:
                    ac.wait_ge(mm_done, START[l, "lora"])
                do(R[0][:, p % 4], yb)
                M("hi")
                point("end")

            def retention(l, h):
                W = lambda e, n: wait_mark(ac, e, l, "rt", h, n)
                M = lambda n: mark(l, "rt", h, n)

                def gate(i):
                    g, f = START[l, f"g{h}"] + i, gate_number(l, h, i)
                    ac.wait_ge(z_out[f % 2], 16 * (f // 2))
                    if h == 0:
                        ac.wait_ge(tmp_used, 40 * l + 8)
                    ac.wait_ge(mm_done, g + 1)
                    ac.activation(halves(ZT[:, f % 2]), two_banks(2 * (g % 2)), ACT.Sigmoid).then_inc(psum_read_a, 1)
                    split_next(g, g % 2)
                W("pe", "tr")
                for b in range(NBLK):
                    do(VT[:, b], ps[:, b, :])
                    M(f"v{b}")
                for b in range(PB):
                    do(KP[:, b], ps[:, 5 + b // 2, 256 * (b % 2):256 * (b % 2) + 256], scale=H_KP[:, b:b + 1])
                do(KP[:, PB], ps[:, 7, 0:256])
                M("k")
                W("pe", "sp")
                if h:
                    ac.wait_ge(kp_out, 16 * (RH * l + h))
                do(SPS, ps[:, 5:7, :])
                M("sp")

                def store_state(b):
                    n = 8 * (RH * l + h) + b
                    W("ve", f"ss{b}")
                    ac.dma_start(outs[7][l, b, h].rearrange("(k p) v -> p k v", p=128),
                                 SR[:, n % 3].rearrange("p (k v) -> p k v", k=2)).then_inc(sr_out[n % 3], 16)
                for b in range(DEC_B - 1):
                    store_state(b)
                W("pe", f"ss{DEC_B - 1}")
                do(Y4[:, :, SEQ:TOK], ps[:, 4, :].rearrange("p (t n) -> p t n", n=128))
                for v in range(4):
                    do(Y4[:, v, 0:SEQ], ps[:, v, :])
                    do(YSQ[:, v], Y4[:, v], ACT.Square)
                    M(f"ysq{v}")
                store_state(DEC_B - 1)
                W("ve", "var")
                do(PT[:, 0:TOK], PT[:, 0:TOK], ACT.Sqrt)
                M("sd")
                gate(0)
                for j in range(2):
                    W("ve", f"y{j}")
                    do(R[0][:, 2 * j:2 * j + 2], Y4[:, 2 * j:2 * j + 2])
                    M(f"hi{j}")
                gate(1)

            split(0, 0, 8)
            split(1, 1, 8)
            for l in range(DEPTH):
                ac.wait_ge(par_in, 13 * 16 * (l + 1))
                do(CR[0:NSTREAM, :], CR[0:NSTREAM, :], ACT.Silu)
                mark(l, "silu")
                wait_mark(ac, "pe", l, "par")
                do(par[:], ps[:, 0, 0:162])
                mark(l, "par")
                wait_mark(ac, "pe", l, "ct")
                do(CT, ps[:, 2, 0:72].rearrange("p (k s) -> p k s", s=NSTREAM))
                mark(l, "ct")
                if l == 0:
                    for b in range(NBLK):
                        wait_mark(ac, "pe", l, f"x{b}")
                        do(X[:, :, 128 * b:128 * b + 128], ps[:, 2 * (b % 4):2 * (b % 4) + 2, :].rearrange("p a (t n) -> p (a t) n", n=128))
                        mark(l, f"x{b}")
                for n in range(12):
                    m = 12 * l + n
                    ac.wait_ge(ada_used, m + 1)
                    if n >= 2:
                        ac.wait_ge(ada_turned, m - 1)
                    do(CR[0:NSTREAM, 512 * (n % 2):512 * (n % 2) + 512], ps[0:NSTREAM, 5 + n % 2, :])
                    ac.sem_inc(ada_row, 1)
                ac.wait_ge(ada_turned, 12 * (l + 1))
                do(mod[:], ps[:, 7, 0:432])
                mark(l, "mod")
                wait_mark(ac, "pe", l, "shr")
                do(psh[:], ps[:, 2, 0:208])
                norm(l, X, S1, "0")
                high_part(l, "0", START[l, "lora"])
                ac.wait_ge(x_out, 16 * (l + 1))
                wait_mark(ac, "ve", l, "h0.3")
                gemm(l, "lora")
                wait_mark(ac, "ve", l, "lora")
                do(ZL[0:64, 0], ZL[0:64, 0], ACT.Tanh)
                do(ZL[:, 1], ZL[:, 1], ACT.Sigmoid)
                mark(l, "lora")
                gemm(l, "rkv0")
                for p in range(PAIRS):
                    rwkv(l, p)
                    if p % 4 == 3:
                        gemm(l, f"ba{p // 4}")
                for i in range(2):
                    f = spill_number(l, PAIRS - 1, Z_TILES[-1] - 2 + i)
                    ac.wait_ge(z_out[f % 2], 16 * (f // 2 + 1))
                gemm(l, "gate0")
                for h in range(RH):
                    retention(l, h)
                    gemm(l, f"bb{h}")
                for j in range(4):
                    wait_mark(ac, "ve", l, f"mg{j}")
                    do(H[0][:, 2 * j:2 * j + 2], ACC[:, 2 * j:2 * j + 2])
                    mark(l, f"mh{j}")
                gemm(l, "out")
                wait_mark(ac, "pe", l, "nsh")
                do(NSR[0:NSTREAM, :], ps[0:NSTREAM].rearrange("p a n -> p (a n)")[:, 0:A_COLS])
                mark(l, "nsh")
                ac.wait_ge(psum_read_v, freed(START[l, "up0"], "v"))
                norm(l, S1, ACC, "m")
                norm(l, X, S1, "1", lambda j: wait_mark(ac, "ve", l, f"xm.{j}"))
                high_part(l, "1", START[l, "up0"])
                wait_mark(ac, "ve", l, "h1.3")
                for f in range(8):
                    gemm(l, f"up{f}")
                    gemm(l, f"down{f}")
                ac.wait_ge(psum_read_v, freed(START[l, "down7"] + 8, "v"))
                norm(l, S1, ACC, "f")
            wait_mark(ac, "ve", DEPTH - 1, "x2")
            ac.wait_ge(sh_out, 32 * DEPTH)
            for b in range(NBLK):
                wait_mark(ac, "pe", DEPTH - 1, f"o{b}")
                do(XR[:, b], ps[:, 2 * (b % 4):2 * (b % 4) + 2, :].rearrange("p a n -> p (a n)"))
                mark(DEPTH - 1, f"o{b}")

        @block.vector
        def _(ve):
            mark_n, order_n = [0], [0]

            def after(ins):
                order_n[0] += 1
                ins.then_inc(ve_order, 1)
                ve.wait_ge(ve_order, order_n[0])

            tt = lambda o, a, b, op: after(ve.tensor_tensor(o, a, b, op))
            ts = lambda o, a, s1, s2, o0, o1=ALU.bypass: after(ve.tensor_scalar(o, a, s1, s2, o0, o1) if s2 is not None else ve.tensor_scalar(o, a, s1, None, o0))
            stt = lambda o, a, s, b, o0, o1: after(ve.scalar_tensor_tensor(o, a, s, b, o0, o1))
            MUL_, ADD, SUB = ALU.mult, ALU.add, ALU.subtract

            def mark(*key):
                mark_n[0] += 1
                assert VEV[key] == mark_n[0], (key, mark_n)
                ve.sem_inc(ve_mark, 1)

            def split(g, s, kt):
                ve.wait_ge(hi_done, g + 1)
                ve.tensor_tensor(WL[:, s, 0:kt], WR[:, s, 0:kt], WH[:, s, 0:kt].bitcast(F32), SUB).then_inc(lo_done, 1)

            cur_kt = [0]

            def split_next(g, s):
                if isinstance(g, int):
                    if g + 2 < TILES:
                        split(g + 2, s, KT[g + 2])
                else:
                    split(g + 2, s, cur_kt[0])

            def gemm(l, name, beside=None):
                g0 = START[l, name]
                n, kt = next((j[1], j[2]) for j in jobs_of_layer() if j[0] == name)
                up0 = 32 * l + (4 * int(name[2:]) if name[:2] == "up" else 0)
                ga0 = freed(g0, "a")
                if name == "gate0":
                    ve.wait_ge(psum_read_v, freed(g0, "v"))

                def tile(g, i, s):
                    par_ = i % 2 if isinstance(i, int) else (s - g0) % 2
                    src = two_banks(2 * s)
                    if name[:2] in ("ba", "bb", "ou", "do"):
                        ve.wait_ge(mm_done, g + 1)
                        dst = halves((ACC if name[0] == "b" else S1)[:, i])
                        if name[-1] == "0" or name == "out":
                            ve.tensor_copy(dst, src).then_inc(psum_read_v, 1)
                        else:
                            ve.wait_ge(psum_read_v, i + (freed(g0, "v") - 7))
                            ve.tensor_tensor(dst, src, dst, ADD).then_inc(psum_read_v, 1)
                    elif name == "gate0":
                        ve.wait_ge(psum_read_a, i + (ga0 + 1))
                        ve.tensor_tensor(ACC[:, i], ACC[:, i], ZT[:, par_], MUL_).then_inc(tmp_used, 1)
                    elif name[:2] == "up":
                        ve.wait_ge(psum_read_a, i + (ga0 + 1))
                        ve.tensor_tensor(FT[:, par_], TM[:, par_], TM[:, par_], MUL_).then_inc(sq_done, 1)
                        ve.wait_ge(sq_done, i + (32 * l + 4 * int(name[2:]) + 1))
                        ve.wait_ge(up_sq, i + (up0 + 1))
                        ve.tensor_tensor(R[1][:, i], FT[:, par_], R[0][:, i].bitcast(F32), SUB).then_inc(tmp_used, 1)

                def both(g, i, s):
                    tile(g, i, s)
                    split_next(g, s)
                    if beside:
                        beside(i)
                if n != 8 or beside:
                    for i in range(n):
                        both(g0 + i, i, (g0 + i) % 2)
                    return
                cur_kt[0] = kt
                for i in range(2):
                    both(g0 + i, i, (g0 + i) % 2)
                with ve.Fori(1, n // 2 - 1) as turn:
                    for s in range(2):
                        both(turn * 2 + (g0 + s), turn * 2 + s, (g0 + s) % 2)
                for i in range(n - 2, n):
                    both(g0 + i, i, (g0 + i) % 2)

            def variance(l, tag, pe_name):
                wait_mark(ve, "pe", l, pe_name)
                ts(halves(RS), two_banks(0), 1.0 / D, EPS, MUL_, ADD)
                mark(l, "var" + tag)
                wait_mark(ve, "ac", l, "sd" + tag)
                after(ve.reciprocal(RS, RS))

            def by_stream(a):
                return a[:, :, SEQ:TOK].rearrange("p k (b t) -> p k b t", t=DEC_T)

            def of_stream(w):
                return w[:, :, 1:NSTREAM, None].to_broadcast([128, 2, DEC_B, DEC_T])

            def pre_norm(l, tag, w, pe_name):
                variance(l, tag, pe_name)
                for j in range(5):
                    if j < 4:
                        two = slice(2 * j, 2 * j + 2)
                        tt(S1[:, two], X[:, two], RS[:, None, :].to_broadcast([128, 2, TOK]), MUL_)
                        tt(by_stream(S1[:, two]), by_stream(S1[:, two]), of_stream(MUL[:, 2 * w, two]), MUL_)
                        tt(by_stream(S1[:, two]), by_stream(S1[:, two]), of_stream(MOD[:, 24 * w + 2 * j:24 * w + 2 * j + 2]), ADD)
                        mark(l, f"hx{tag}.{j}")
                    if j:
                        wait_mark(ve, "ac", l, f"hi{tag}.{j - 1}")
                        two = slice(2 * j - 2, 2 * j)
                        tt(H[1][:, two], S1[:, two], H[0][:, two].bitcast(F32), SUB)
                        mark(l, f"h{tag}.{j - 1}")

            def post_norm(l, tag, w, pe_name, done):
                variance(l, tag, pe_name)
                for j in range(4):
                    two = slice(2 * j, 2 * j + 2)
                    tt(S1[:, two], S1[:, two], RS[:, None, :].to_broadcast([128, 2, TOK]), MUL_)
                    for t in (2 * j, 2 * j + 1):
                        stt(X[:, t, 0:SEQ], S1[:, t, 0:SEQ], MUL[:, 2 * w + 1, t, 0:1], X[:, t, 0:SEQ], MUL_, ADD)
                    tt(by_stream(S1[:, two]), by_stream(S1[:, two]), of_stream(MUL[:, 2 * w + 1, two]), MUL_)
                    tt(by_stream(X[:, two]), by_stream(X[:, two]), by_stream(S1[:, two]), ADD)
                    mark(l, f"x{tag}.{j}")
                mark(l, done)

            def token_shift(z, t):
                after(ve.tensor_copy(NSH[:, t, 0:1], z[:, SEQ - 1:SEQ]))
                after(ve.tensor_copy(NSH[:, t, 1:NSTREAM], z[:, SEQ + DEC_T - 1:TOK:DEC_T]))
                tt(t1[:, 1:TOK], z[:, 0:TOK - 1], z[:, 1:TOK], SUB)
                ts(t1[:, 0:1], z[:, 0:1], -1.0, None, MUL_)
                tt(t1[:, SEQ:TOK:DEC_T], PSH[:, t], z[:, SEQ:TOK:DEC_T], SUB)
                stt(z, t1, par[:, P_MU + t:P_MU + t + 1], z, MUL_, ADD)

            def rwkv(l, p):
                W = lambda e, n: wait_mark(ve, e, l, "rw", p, n)
                M = lambda n: mark(l, "rw", p, n)
                col = lambda c: par[:, c + p:c + p + 1]
                tiles_ = filler(l, p)

                def beside(i, q):
                    if q == 3:
                        g = tiles_[i][0]
                        split_next(g, g % 2)
                point = part_of(l, p, beside)
                if p:
                    ve.wait_ge(z_in, 16 * ((PAIRS - 1) * l + p))
                else:
                    ve.wait_ge(psum_read_a, freed(START[l, "rkv0"] + 3, "a"))
                for i, z in enumerate((r_b, k_b, v_b)):
                    token_shift(z, 8 * i + p)
                M("mix")
                ts(kk, k_b, col(P_KK), None, MUL_)
                tt(t1, kk, kk, MUL_)
                M("sq")
                point("sq")
                W("ac", "sig")
                ts(lam, lam, -float(np.exp(-0.5)), None, MUL_)
                after(ve.tensor_tensor_scan(cu, c1[:, C_RM:C_RM + TOK], lam, 0.0, MUL_, ADD))
                W("ac", "nr")
                ts(t1, t1, 1e-12, None, ALU.max)
                after(ve.reciprocal(t1, t1))
                tt(kk, kk, t1, MUL_)
                ts(t1, ic, -1.0, col(P_KA), ADD, MUL_)
                stt(k_b, t1, 1.0, k_b, ADD, MUL_)
                stt(t1, r_b, col(P_RK), k_b, MUL_, MUL_)
                M("rk")
                point("rk")
                W("pe", "bs")
                tt(halves(bo), two_banks(2), halves(v_b), MUL_)
                M("bo")
                after(ve.tensor_copy(MID, cu[:, 63:SEQ:128]))
                cp = cu[:, 0:SEQ].rearrange("p (c n) -> p c n", n=128)
                tt(cp, cp, MID[:, :, None].to_broadcast([128, PB, 128]), SUB)
                tt(t1, cu, lam, SUB)
                M("ea")
                tt(ic, ic, kk, MUL_)
                W("ac", "ea")
                stt(kk, kk, -1.0, t1, MUL_, MUL_)
                W("ac", "exp")
                tt(ic, ic, lam, MUL_)
                tt(k_b, k_b, lam, MUL_)
                tt(r_b, r_b, cu, MUL_)
                after(ve.tensor_copy(PC[:, 0:PB], cu[:, 127:SEQ:128]))
                after(ve.tensor_copy(PC[:, PB:PB + DEC_B], cu[:, SEQ + DEC_T - 1:TOK:DEC_T]))
                for q in range(2):
                    hm = c1[:, C_HM + q:C_HM + q + 1]
                    ts(ATR[:, :, 128 * q:128 * q + 128], kk.rearrange("p (c n) -> p c n", n=128), hm, None, MUL_)
                    ts(ATR[:, :, 256 + 128 * q:256 + 128 * q + 128], r_b.rearrange("p (c n) -> p c n", n=128), hm, None, MUL_)
                M("abkr")
                point("ab")
                for j in range(2 * NBLK):
                    b, bank = j // 2, (2, 3, 6, 7)[j % 4]
                    W("pe", f"s{j}")
                    strict, incl = (C_SUS, C_IUS) if b == PB else (C_SU, C_IU)
                    src = ps[:, bank, :].rearrange("p (t n) -> p t n", n=128)
                    for part, (dst, mk) in enumerate((((LTI, AKT)[j % 2], strict), ((BRT, KRT)[j % 2], incl))):
                        tt(dst[:, 2 * b:2 * b + 2], src[:, 2 * part:2 * part + 2],
                           c1[:, None, mk:mk + 128].to_broadcast([128, 2, 128]), MUL_)
                    M(f"s{j}")
                point("z")
                tt(LTI, LTI, ident[:, None, :].to_broadcast([128, 2 * NBLK, 128]), ADD)
                M("lti")
                point("lti")
                for g in range(3):
                    W("pe", f"lt{g}")
                    n = 2 if g == 2 else 4
                    sl = slice(4 * g, 4 * g + n)
                    bc = lambda c: c1[:, None, c:c + 128].to_broadcast([128, n, 128])
                    tt(XM[:, sl], ps[:, 2 + g, 0:128 * n].rearrange("p (t n) -> p t n", n=128), bc(C_LM), MUL_)
                    tt(XTM[:, sl], LTI[:, sl], bc(C_LMT), MUL_)
                    M(f"x0.{g}")
                for lv in range(1, LEVELS):
                    for g in rw_groups(lv):
                        W("pe", f"T{lv}.{g}")
                        n = 2 if g == 2 else 4
                        c = C_LM + 128 * lv
                        if lv == 1:
                            W("pe", "z")
                        tt(T1[:, 4 * g:4 * g + n], ps[:, 2 + g, 0:128 * n].rearrange("p (t n) -> p t n", n=128),
                           c1[:, None, c:c + 128].to_broadcast([128, n, 128]), MUL_)
                        M(f"T{lv}.{g}")
                    point(f"la{lv}")
                    point(f"lb{lv}")
                point("uw")
                for c in range(PB):
                    if c:
                        ts(SS, S, EM[:, c:c + 1], None, MUL_)
                        M(f"ss{c}")
                        W("pe", f"u{c}")
                        tt(U[:, c], ps[:, 4, 0:128], U0[:, c], ADD)
                    else:
                        W("ac", "uw")
                        after(ve.tensor_copy(U[:, 0], U0[:, 0]))
                    M(f"u{c}")
                    W("pe", f"new{c}")
                    tt(TN, ps[:, 5, 0:128], bones, MUL_)
                    if c:
                        tt(TN, TN, SS, ADD)
                    ts(S, TN, PC[:, c:c + 1], None, MUL_)
                    M(f"new{c}")
                    point(f"ca{c}")
                    point(f"cb{c}")
                e8 = c1[:, C_E8:C_E8 + 64].rearrange("p (b c) -> p b c", c=DEC_B)[:, :, :, None].to_broadcast([128, DEC_B, DEC_B, DEC_T])

                def alone(dst, src):
                    a = src.rearrange("p (c n) -> p c n", n=DEC_T)[:, None, :, :].to_broadcast([128, DEC_B, DEC_B, DEC_T])
                    tt(dst.rearrange("p b (c n) -> p b c n", n=DEC_T), a, e8, MUL_)
                alone(WM, WT[:, PB])
                M("wm")
                alone(RM, r_b[:, SEQ:TOK])
                for b in range(DEC_B):
                    bm = c1[:, C_BM + b:C_BM + b + 1]
                    ts(BKM[:, b], TOKB[:, 4 * PB + 1], bm, None, MUL_)
                    ts(BKM[:, 8 + b], TOKB[:, 4 * PB + 2], bm, None, MUL_)
                M("smask")
                W("pe", "su")
                tt(U[:, PB], ps[:, 5, 128:256], U0[:, PB], ADD)
                M("su")
                point("su")
                W("pe", "snew")
                tt(TNS, ps[:, 2:4, :].rearrange("p a (t n) -> p (a t) n", n=128), bones[:, None, :].to_broadcast([128, DEC_B, 128]), MUL_)
                tt(TNS, TNS, STS, ADD)
                tt(TNS, TNS, PC[:, PB:PB + DEC_B, None].to_broadcast([128, DEC_B, 128]), MUL_)
                M("snew")
                point("sn")
                W("pe", "gn1")
                stt(halves(yb), two_banks(2), -1.0 / 64, halves(yb), MUL_, ADD)
                tt(t1, yb, yb, MUL_)
                M("yc")
                point("so")
                W("pe", "gn2")
                ts(halves(t1), two_banks(4), 1.0 / 64, GN_EPS, MUL_, ADD)
                M("var")
                point("gn")
                W("ac", "sd")
                after(ve.reciprocal(t1, t1))
                tt(yb, yb, t1, MUL_)
                ts(yb, yb, col(P_LW), col(P_LB), MUL_, ADD)
                tt(yb, yb, bo, ADD)
                tt(yb, yb, gt, MUL_)
                M("y")
                W("ac", "hi")
                tt(R[1][:, p % 4], yb, R[0][:, p % 4].bitcast(F32), SUB)
                M("split")
                point("end")

            def rope(l, h):
                def begin():
                    ve.wait_ge(qk_in, 16 * (RH * l + h + 1))
                    ve.wait_ge(ret_in, 16 * ((RH * l + h + 1) * len(HEAD_CONSTS) + l + 1))
                yield begin
                for j in (0, 2):
                    x1, x2 = QKV[:, j], QKV[:, j + 1]
                    yield lambda x1=x1, x2=x2: tt(RT1[:, 0], x2, sinT, MUL_)
                    yield lambda x1=x1, x2=x2: tt(RT1[:, 1], x1, sinT, MUL_)
                    yield lambda x1=x1, x2=x2: tt(x1, x1, cosT, MUL_)
                    yield lambda x1=x1, x2=x2: tt(x2, x2, cosT, MUL_)
                    yield lambda x1=x1, x2=x2: tt(x1, x1, RT1[:, 0], SUB)
                    yield lambda x1=x1, x2=x2: tt(x2, x2, RT1[:, 1], ADD)

                def end():
                    by_stream_token = lambda a: a.rearrange("p k (b t) -> p k b t", t=DEC_T)
                    tt(by_stream_token(QD), by_stream_token(QKV[:, 0:2, SEQ:TOK]), H_QD[:, None, None, :].to_broadcast([128, 2, DEC_B, DEC_T]), MUL_)
                    mark(l, "rt", h, "rope")
                yield end

            def retention(l, h):
                W = lambda e, n: wait_mark(ve, e, l, "rt", h, n)
                M = lambda n: mark(l, "rt", h, n)
                W("ac", "k")
                for b in range(DEC_B):
                    ts(KS[:, b], KP[:, PB].rearrange("p (k n) -> p k n", n=128), H_KS[:, b:b + 1], None, MUL_)
                M("ks")
                at_ = 0
                for b in range(NBLK):
                    W("pe", f"s{b}")
                    n = SEQ - 128 * b if b < PB else 128
                    tt(PT[:, at_:at_ + n], ps[:, b, 0:n], H_MW[:, 0:n] if b < PB else H_MS, MUL_)
                    at_ += n
                    M(f"p{b}")
                e8 = c1[:, C_E8:C_E8 + 64].rearrange("p (b c) -> p b c", c=DEC_B)[:, :, :, None].to_broadcast([128, DEC_B, DEC_B, DEC_T])
                for k in range(2):
                    a = QD[:, k].rearrange("p (c n) -> p c n", n=DEC_T)[:, None, :, :].to_broadcast([128, DEC_B, DEC_B, DEC_T])
                    tt(QX[:, k].rearrange("p b (c n) -> p b c n", n=DEC_T), a, e8, MUL_)
                M("qx")
                g16 = float((1.0 - 2.0 ** (-5.0 - h)) ** DEC_T)
                for b in range(DEC_B):
                    n = 8 * (RH * l + h) + b
                    W("pe", f"ss{b}")
                    s = SR[:, n % 3].rearrange("p (k v) -> p k v", k=2)
                    stt(s, s, g16, ps[:, 5:7, :], MUL_, ADD)
                    M(f"ss{b}")
                W("pe", "rn")
                ts(halves(PT[:, 0:TOK]), two_banks(5), 1.0 / RV, EPS, MUL_, ADD)
                M("var")
                W("ac", "sd")
                after(ve.reciprocal(PT[:, 0:TOK], PT[:, 0:TOK]))
                tt(Y4, Y4, PT[:, None, 0:TOK].to_broadcast([128, 4, TOK]), MUL_)
                split_next(START[l, f"g{h}"], START[l, f"g{h}"] % 2)
                for j in range(2):
                    two = slice(2 * j, 2 * j + 2)
                    tt(Y4[:, two], Y4[:, two], SG[:, two], MUL_)
                    M(f"y{j}")
                for j in range(2):
                    two = slice(2 * j, 2 * j + 2)
                    W("ac", f"hi{j}")
                    tt(R[1][:, two], Y4[:, two], R[0][:, two].bitcast(F32), SUB)
                    M("split" if j else "split0")
                split_next(START[l, f"g{h}"] + 1, 1 - START[l, f"g{h}"] % 2)

            split(0, 0, 8)
            split(1, 1, 8)
            ve.wait_ge(const_in, 16)
            for l in range(DEPTH):
                wait_mark(ve, "ac", l, "mod")
                tt(MOD, MOD, par[:, P_ADA:P_ADA + 48, None].to_broadcast([128, 48, NSTREAM]), ADD)
                for w in range(2):
                    npre = par[:, P_PRE + 8 * w:P_PRE + 8 * w + 8, None].to_broadcast([128, KD, NSTREAM])
                    npost = par[:, P_POST + 8 * w:P_POST + 8 * w + 8, None].to_broadcast([128, KD, NSTREAM])
                    stt(MUL[:, 2 * w], MOD[:, 24 * w + 8:24 * w + 16], 1.0, npre, ADD, MUL_)
                    tt(MUL[:, 2 * w + 1], MOD[:, 24 * w + 16:24 * w + 24], npost, MUL_)
                mark(l, "mod")
                pre_norm(l, "0", 0, "n0")
                gemm(l, "lora")
                ve.wait_ge(psum_read_a, freed(START[l, "rkv0"], "a"))
                token_shift(ZL[:, 0], 24)
                token_shift(ZL[:, 1], 25)
                mark(l, "lora")
                gemm(l, "rkv0")
                for p in range(PAIRS):
                    rwkv(l, p)
                    if p % 4 == 3:
                        gemm(l, f"ba{p // 4}")
                for step in rope(l, 0):
                    step()
                gemm(l, "gate0")
                for h in range(RH):
                    retention(l, h)
                    if h == 0:
                        ve.wait_ge(m_out, 16 * (l + 1))
                    if h == RH - 1:
                        gemm(l, f"bb{h}")
                        break
                    steps = list(rope(l, h + 1))

                    def beside(i):
                        for step in steps[2 * i:2 * i + 2]:
                            step()
                    gemm(l, f"bb{h}", beside)
                ve.wait_ge(m_in, 32 * KD * (l + 1))
                ve.wait_ge(psum_read_v, freed(START[l, "out"], "v"))

                def low_part(j):
                    wait_mark(ve, "ac", l, f"mh{j}")
                    tt(H[1][:, 2 * j:2 * j + 2], ACC[:, 2 * j:2 * j + 2], H[0][:, 2 * j:2 * j + 2].bitcast(F32), SUB)
                    mark(l, f"ms{j}")
                for j in range(4):
                    two = slice(2 * j, 2 * j + 2)
                    tt(ACC[:, two], ACC[:, two], G1[:, two], MUL_)
                    tt(ACC[:, two], ACC[:, two], MS[:, two], ADD)
                    mark(l, f"mg{j}")
                    if j:
                        low_part(j - 1)
                low_part(3)
                gemm(l, "out")
                ve.wait_ge(x_back, 16 * (l + 1))
                post_norm(l, "m", 0, "mix", "x1")
                pre_norm(l, "1", 1, "n1")
                for f in range(8):
                    gemm(l, f"up{f}")
                    gemm(l, f"down{f}")
                post_norm(l, "f", 1, "ffn", "x2")


_INS = ['x_prompt', 'x_sample', 'state_shift', 'state_rwkv', 'state_ret', 'c_prompt', 'c_sample', 'ada_w', 'ada_b', 'norm_pre',
        'norm_post', 'w_in', 'a_mu', 'a_w0', 'a_w2', 'a_a0', 'a_a2', 'a_g2', 'a_kk', 'a_ka', 'a_rk', 'a_ln_w', 'a_ln_b',
        'w_branch_a', 'w_branch_b', 'w_out', 'w_ffn_up', 'w_ffn_down']
_OUTS = [(1, SEQ, D), (DEC_B, DEC_T, D), (DEPTH, 1, A_COLS), (DEPTH, 1, 16, 64, 64), (DEPTH, 1, RH, RK, RV),
         (DEPTH, DEC_B, A_COLS), (DEPTH, DEC_B, 16, 64, 64), (DEPTH, DEC_B, RH, RK, RV)]


def program(nc, shapes):
    io = {n: nc.dram_tensor(f"in_{n}_dram", s, F32, kind="ExternalInput").ap() for n, s in shapes.items()}
    outs = [nc.dram_tensor(f"out_{i}_dram", s, F32, kind="ExternalOutput").ap() for i, s in enumerate(_OUTS)]
    scratch = {n: nc.dram_tensor(f"scratch_{n}", (128, KD, TOK), F32, kind="Internal").ap() for n in ("x", "m")}
    scratch["z"] = nc.dram_tensor("scratch_z", (SPILLED, 128, TOK), F32, kind="Internal").ap()
    build(nc, io, outs, scratch)


def kernel(**inputs):
    import concourse.bacc as _bacc
    from concourse.bass_utils import run_bass_kernel_spmd as _run

    nc = _bacc.Bacc("TRN2", target_bir_lowering=False, num_devices=1)
    arrays = {n: np.ascontiguousarray(inputs[n]) for n in _INS}
    arrays["const1"], arrays["const2"] = shape_constants()
    program(nc, {n: a.shape for n, a in arrays.items()})
    r = _run(nc, [{f"in_{n}_dram": a for n, a in arrays.items()}], core_ids=[0])
    return tuple(r.results[0][f"out_{i}_dram"] for i in range(len(_OUTS)))
```
